# Optimizing a Trainium2 kernel written in Bass

```python
import jax, jax.numpy as jnp
from jax import lax
import numpy as np
import math

D_MODEL = 1024
BATCH = 1
SEQ = 256
DEPTH = 2

HGRN_HEADS = 8
HGRN_EXPAND = 128
HGRN_VDIM = 128
HGRN_KEY_WIDTH = HGRN_HEADS * HGRN_EXPAND
HGRN_VAL_WIDTH = HGRN_HEADS * HGRN_VDIM
HGRN_SCALE = HGRN_EXPAND ** -0.5
CHUNK = 64
F_MIN = 1e-6
CONV_CH = D_MODEL
CONV_K = 3
D_FF = 2816
N_EXPERTS = 8
TOP_K = 2
EPS = 1e-6
N_DENSE = (DEPTH + 1) // 2
N_MOE = DEPTH // 2
IN_SPLITS = (HGRN_KEY_WIDTH, HGRN_KEY_WIDTH, HGRN_VAL_WIDTH, HGRN_VAL_WIDTH,
             CONV_CH, CONV_CH, CONV_CH, D_MODEL, D_MODEL)
IN_WIDTH = sum(IN_SPLITS)


def rms_norm(x, w):
    xf = x.astype(jnp.float32)
    y = xf * lax.rsqrt(jnp.mean(xf * xf, axis=-1, keepdims=True) + EPS)
    return (y * w.astype(jnp.float32)).astype(x.dtype)

def split_projection(h, w):
    outs = []
    start = 0
    for width in IN_SPLITS:
        outs.append(jnp.einsum('bsd,de->bse', h, w[:, start:start + width]))
        start += width
    return outs

def hgrn2_chunk_recurrence(q, k, v, log_f):
    bsz, seq, nh, kd = q.shape
    vd = v.shape[-1]
    n_chunks = seq // CHUNK

    def to_chunks(t):
        return t.reshape(bsz, n_chunks, CHUNK, nh, t.shape[-1]).transpose(1, 0, 3, 2, 4)

    causal = jnp.tril(jnp.ones((CHUNK, CHUNK), dtype=bool))[:, :, None]

    def step(state, inp):
        qc, kc, vc, gc = inp
        cum = jnp.cumsum(gc, axis=2)
        diff = cum[:, :, :, None, :] - cum[:, :, None, :, :]
        decay = jnp.where(causal, jnp.exp(jnp.where(causal, diff, 0.0)), 0.0)
        scores = jnp.einsum('bhtk,bhtsk,bhsk->bhts', qc, decay, kc)
        o = (jnp.einsum('bhts,bhsv->bhtv', scores, vc)
             + jnp.einsum('bhtk,bhkv->bhtv', qc * jnp.exp(cum), state))
        last = cum[:, :, -1:, :]
        state = (jnp.exp(last[:, :, 0, :])[..., None] * state
                 + jnp.einsum('bhsk,bhsv->bhkv', kc * jnp.exp(last - cum), vc))
        return state, o

    s0 = jnp.zeros((bsz, nh, kd, vd), jnp.float32)
    _, o = lax.scan(step, s0, (to_chunks(q), to_chunks(k), to_chunks(v), to_chunks(log_f)))
    return o.transpose(1, 0, 3, 2, 4).reshape(bsz, seq, nh, vd)

def hybrid_mixer(h, w_in, lb, g_norm_w, conv_w, w_proj_hgrn, w_proj_conv, w_out):
    bsz, seq, _ = h.shape
    q, f_logit, i_in, g_out, b_gate, c_gate, u, gate_a, gate_b = split_projection(h, w_in)

    def heads(t):
        return t.reshape(bsz, seq, HGRN_HEADS, -1).astype(jnp.float32)

    z = heads(f_logit)
    lbh = lb.astype(jnp.float32).reshape(HGRN_HEADS, HGRN_EXPAND)
    f = lbh + (1.0 - lbh) * jax.nn.sigmoid(z)
    log_f = jnp.log(jnp.maximum(f, F_MIN))
    k = (1.0 - lbh) * jax.nn.sigmoid(-z)
    qh = jax.nn.silu(heads(q)) * HGRN_SCALE
    o = hgrn2_chunk_recurrence(qh, k, heads(i_in), log_f)
    o = rms_norm(o, g_norm_w) * jax.nn.silu(heads(g_out))
    y_a = jnp.einsum('bse,ed->bsd', o.reshape(bsz, seq, HGRN_VAL_WIDTH).astype(h.dtype), w_proj_hgrn)

    v = b_gate * u
    vp = jnp.pad(v, ((0, 0), (CONV_K - 1, 0), (0, 0)))
    conv = conv_w[0] * vp[:, 0:seq, :]
    for j in range(1, CONV_K):
        conv = conv + conv_w[j] * vp[:, j:j + seq, :]
    y_b = jnp.einsum('bse,ed->bsd', c_gate * conv, w_proj_conv)

    merged = jax.nn.sigmoid(gate_a) * y_a + jax.nn.sigmoid(gate_b) * y_b
    return jnp.einsum('bsd,de->bse', merged, w_out)

def swiglu(h, w1, w3, w2):
    a = jnp.einsum('bsd,df->bsf', h, w1)
    b = jnp.einsum('bsd,df->bsf', h, w3)
    return jnp.einsum('bsf,fd->bsd', jax.nn.silu(a) * b, w2)

def moe_swiglu(h, router_w, w1, w3, w2):
    bsz, seq, d = h.shape
    t = h.reshape(bsz * seq, d)
    logits = jnp.einsum('td,de->te', t, router_w).astype(jnp.float32)
    top_vals, top_idx = lax.top_k(logits, TOP_K)
    top_w = jax.nn.softmax(top_vals, axis=-1)
    gates = jnp.sum(jax.nn.one_hot(top_idx, N_EXPERTS, dtype=jnp.float32) * top_w[..., None], axis=1)
    gates = gates.astype(h.dtype)
    out = jnp.zeros_like(t)
    for e in range(N_EXPERTS):
        a = t @ w1[e]
        b = t @ w3[e]
        out = out + gates[:, e:e + 1] * ((jax.nn.silu(a) * b) @ w2[e])
    return out.reshape(bsz, seq, d)

def first_inputs(seed: int = 0) -> dict:
    key = jax.random.key(seed)
    ks = jax.random.split(key, 20)
    nrm = lambda k, shape, fan_in: jax.random.normal(k, shape, jnp.float32) * (fan_in ** -0.5)
    gain = lambda k, shape: 1.0 + 0.05 * jax.random.normal(k, shape, jnp.float32)
    return {
        "x": jax.random.normal(ks[0], (BATCH, SEQ, D_MODEL), jnp.float32),
        "w_in": nrm(ks[1], (DEPTH, D_MODEL, IN_WIDTH), D_MODEL),
        "lower_bounds": 0.1 * jax.random.normal(ks[2], (DEPTH, HGRN_KEY_WIDTH), jnp.float32),
        "hgrn_norm_w": gain(ks[3], (DEPTH, HGRN_VDIM)),
        "conv_w": nrm(ks[4], (DEPTH, CONV_K, CONV_CH), CONV_K),
        "w_proj_hgrn": nrm(ks[5], (DEPTH, HGRN_VAL_WIDTH, D_MODEL), HGRN_VAL_WIDTH),
        "w_proj_conv": nrm(ks[6], (DEPTH, CONV_CH, D_MODEL), CONV_CH),
        "w_out": nrm(ks[7], (DEPTH, D_MODEL, D_MODEL), D_MODEL),
        "norm_mix": gain(ks[8], (DEPTH, D_MODEL)),
        "norm_ffn": gain(ks[9], (DEPTH, D_MODEL)),
        "dense_w1": nrm(ks[10], (N_DENSE, D_MODEL, D_FF), D_MODEL),
        "dense_w3": nrm(ks[11], (N_DENSE, D_MODEL, D_FF), D_MODEL),
        "dense_w2": nrm(ks[12], (N_DENSE, D_FF, D_MODEL), D_FF),
        "router_w": nrm(ks[13], (N_MOE, D_MODEL, N_EXPERTS), D_MODEL),
        "expert_w1": nrm(ks[14], (N_MOE, N_EXPERTS, D_MODEL, D_FF), D_MODEL),
        "expert_w3": nrm(ks[15], (N_MOE, N_EXPERTS, D_MODEL, D_FF), D_MODEL),
        "expert_w2": nrm(ks[16], (N_MOE, N_EXPERTS, D_FF, D_MODEL), D_FF),
        "final_norm": gain(ks[17], (D_MODEL,)),
    }

def first_block(x, w_in, lower_bounds, hgrn_norm_w, conv_w, w_proj_hgrn, w_proj_conv, w_out,
              norm_mix, norm_ffn, dense_w1, dense_w3, dense_w2, router_w,
              expert_w1, expert_w3, expert_w2, final_norm):
    lb_soft = jax.nn.softmax(lower_bounds.astype(jnp.float32), axis=0)
    lb_all = jnp.cumsum(lb_soft, axis=0) - lb_soft[0]
    for layer in range(DEPTH):
        h = rms_norm(x, norm_mix[layer])
        x = x + hybrid_mixer(h, w_in[layer], lb_all[layer], hgrn_norm_w[layer], conv_w[layer],
                             w_proj_hgrn[layer], w_proj_conv[layer], w_out[layer])
        h = rms_norm(x, norm_ffn[layer])
        if layer % 2 == 0:
            j = layer // 2
            x = x + swiglu(h, dense_w1[j], dense_w3[j], dense_w2[j])
        else:
            j = layer // 2
            x = x + moe_swiglu(h, router_w[j], expert_w1[j], expert_w3[j], expert_w2[j])
    return rms_norm(x, final_norm)


N_BRANCH = 4
BRANCH_W = 256
GM_GROUPS = 4
GM_CHUNK = 128
GM_GD = BRANCH_W // GM_GROUPS
POOL_WINDOWS = (2, 4, 8, 16)
POOL_GD = BRANCH_W // len(POOL_WINDOWS)
ATT_HEADS = 4
ATT_HD = BRANCH_W // ATT_HEADS
IDX_HEADS = 4
IDX_HD = 32
TOPK_MAX = 256
Q_BLOCK = 128
REL_BUCKETS = 32
REL_MAX_DIST = 128
CONV_K_2 = 31

IN_SIZES = (2 * BRANCH_W, BRANCH_W, BRANCH_W, BRANCH_W, BRANCH_W, IDX_HEADS * IDX_HD, IDX_HD, IDX_HEADS, 2 * BRANCH_W, N_BRANCH * D_MODEL)
IN_COLS = 2 * BRANCH_W + 4 * BRANCH_W + IDX_HEADS * IDX_HD + IDX_HD + IDX_HEADS + 2 * BRANCH_W + N_BRANCH * D_MODEL


def rmsnorm(x, g):
    xf = x.astype(jnp.float32)
    y = xf * lax.rsqrt(jnp.mean(xf * xf, axis=-1, keepdims=True) + EPS)
    return (y * g.astype(jnp.float32)).astype(x.dtype)

def layernorm(x, g, b):
    xf = x.astype(jnp.float32)
    mu = jnp.mean(xf, axis=-1, keepdims=True)
    xc = xf - mu
    y = xc * lax.rsqrt(jnp.mean(xc * xc, axis=-1, keepdims=True) + EPS)
    return (y * g.astype(jnp.float32) + b.astype(jnp.float32)).astype(x.dtype)

def swiglu_ffn(h, w_gu, w_down):
    a, b = jnp.split(h @ w_gu, 2, axis=-1)
    return (jax.nn.silu(a) * b) @ w_down

def gmlp_mixer(uv, v_g, ws, wb):
    B, S, _ = uv.shape
    u, v = jnp.split(jax.nn.gelu(uv), 2, axis=-1)
    v = rmsnorm(v, v_g)
    vc = v.reshape(B, S // GM_CHUNK, GM_CHUNK, GM_GROUPS, GM_GD)
    causal = jnp.tril(jnp.ones((GM_CHUNK, GM_CHUNK), dtype=bool))
    wsm = jnp.where(causal[None], ws, 0.0).astype(v.dtype)
    mixed = jnp.einsum('gts,bcsgd->bctgd', wsm, vc) + wb.T[None, None, :, :, None]
    return u * mixed.reshape(B, S, BRANCH_W)

def pool_mixer(p, pw, scale):
    B, S, _ = p.shape
    wmax = POOL_WINDOWS[-1]
    pf = p.astype(jnp.float32)
    csp = jnp.pad(jnp.cumsum(pf, axis=1), ((0, 0), (wmax, 0), (0, 0)))
    count = jnp.arange(1, S + 1, dtype=jnp.float32)[:, None]
    outs = []
    for g, w in enumerate(POOL_WINDOWS):
        sl = slice(g * POOL_GD, (g + 1) * POOL_GD)
        win = csp[:, wmax:, sl] - csp[:, wmax - w:wmax - w + S, sl]
        outs.append(win / jnp.minimum(count, float(w)) - pf[:, :, sl])
    d = jnp.stack(outs, axis=2).astype(p.dtype)
    y = jnp.einsum('bsgc,gcd->bsgd', d, pw).reshape(B, S, BRANCH_W)
    return y * scale

def conv_mixer(ab, dw, db, ln_g, ln_b):
    a, gt = jnp.split(ab, 2, axis=-1)
    h = a * jax.nn.sigmoid(gt)
    h = lax.conv_general_dilated(h, dw[:, None, :].astype(h.dtype), window_strides=(1,),
                                 padding=[(CONV_K_2 - 1, 0)], dimension_numbers=('NWC', 'WIO', 'NWC'),
                                 feature_group_count=BRANCH_W) + db
    return jax.nn.silu(layernorm(h, ln_g, ln_b))

def t5_bucket(n):
    n = jnp.maximum(n, 0)
    max_exact = REL_BUCKETS // 2
    large = max_exact + (jnp.log(jnp.maximum(n, 1).astype(jnp.float32) / max_exact)
                         / math.log(REL_MAX_DIST / max_exact) * (REL_BUCKETS - max_exact)).astype(jnp.int32)
    return jnp.where(n < max_exact, n, jnp.minimum(large, REL_BUCKETS - 1))

def sparse_attention(q, k, v, q_idx, k_idx, w_idx, rel_bias):
    B, S, _ = q.shape
    topk = min(TOPK_MAX, S // 4)
    q = q.reshape(B, S, ATT_HEADS, ATT_HD)
    k = k.reshape(B, S, ATT_HEADS, ATT_HD)
    v = v.reshape(B, S, ATT_HEADS, ATT_HD)
    q_idx = q_idx.reshape(B, S, IDX_HEADS, IDX_HD)
    w_idx = w_idx.astype(jnp.float32) * (IDX_HEADS ** -0.5)
    s_pos = jnp.arange(S)
    gather = jax.vmap(lambda a, i: a[i])

    def block(i):
        t0 = i * Q_BLOCK
        t_pos = t0 + jnp.arange(Q_BLOCK)
        qb = lax.dynamic_slice_in_dim(q, t0, Q_BLOCK, axis=1)
        qib = lax.dynamic_slice_in_dim(q_idx, t0, Q_BLOCK, axis=1)
        wib = lax.dynamic_slice_in_dim(w_idx, t0, Q_BLOCK, axis=1)
        rel = jax.nn.relu(jnp.einsum('bqhd,bsd->bqhs', qib, k_idx).astype(jnp.float32) * (IDX_HD ** -0.5))
        score = jnp.einsum('bqh,bqhs->bqs', wib, rel)
        score = jnp.where(s_pos[None, None, :] <= t_pos[None, :, None], score, -jnp.inf)
        _, idx = lax.top_k(score, topk)
        valid = idx <= t_pos[None, :, None]
        ks = gather(k, idx)
        vs = gather(v, idx)
        bias = rel_bias[t5_bucket(t_pos[None, :, None] - idx)]
        logits = (jnp.einsum('bqhd,bqkhd->bqhk', qb, ks).astype(jnp.float32) * (ATT_HD ** -0.5)
                  + bias.astype(jnp.float32).transpose(0, 1, 3, 2))
        logits = jnp.where(valid[:, :, None, :], logits, -jnp.inf)
        p = jax.nn.softmax(logits, axis=-1).astype(v.dtype)
        o = jnp.einsum('bqhk,bqkhd->bqhd', p, vs)
        return o.reshape(B, Q_BLOCK, BRANCH_W)

    out = lax.map(block, jnp.arange(S // Q_BLOCK))
    return out.transpose(1, 0, 2, 3).reshape(B, S, BRANCH_W)

def mixing_sublayer(h, w_in, gm_v_g, gm_ws, gm_b, pool_w, pool_scale, conv_dw, conv_b,
                    conv_ln_g, conv_ln_b, w_branch, w_out, rel_bias):
    B, S, _ = h.shape
    z = h @ w_in
    uv, pz, qz, kz, vz, qi, ki, wi, cz, gz = jnp.split(z, list(np.cumsum(IN_SIZES)[:-1]), axis=-1)
    branches = (
        gmlp_mixer(uv, gm_v_g, gm_ws, gm_b),
        pool_mixer(pz, pool_w, pool_scale),
        sparse_attention(qz, kz, vz, qi, ki, wi, rel_bias),
        conv_mixer(cz, conv_dw, conv_b, conv_ln_g, conv_ln_b),
    )
    gates = jax.nn.sigmoid(gz.reshape(B, S, N_BRANCH, D_MODEL))
    y = gates[:, :, 0] * (branches[0] @ w_branch[0])
    for n in range(1, N_BRANCH):
        y = y + gates[:, :, n] * (branches[n] @ w_branch[n])
    return y @ w_out

def second_inputs(seed: int = 0) -> dict:
    key = jax.random.key(seed)
    ks = jax.random.split(key, 24)
    f32 = jnp.float32

    def nrm(k, shape, scale):
        return jax.random.normal(k, shape, f32) * scale

    def gain(k, shape):
        return 1.0 + 0.05 * jax.random.normal(k, shape, f32)

    L, D, C, F = DEPTH, D_MODEL, BRANCH_W, D_FF
    return {
        'x': nrm(ks[0], (BATCH, SEQ, D), 1.0),
        'ffn1_pre_g': gain(ks[1], (L, D)),
        'ffn1_post_g': gain(ks[2], (L, D)),
        'ffn1_w_gu': nrm(ks[3], (L, D, 2 * F), D ** -0.5),
        'ffn1_w_down': nrm(ks[4], (L, F, D), F ** -0.5),
        'mix_pre_g': gain(ks[5], (L, D)),
        'mix_post_g': gain(ks[6], (L, D)),
        'w_in': nrm(ks[7], (L, D, IN_COLS), D ** -0.5),
        'gm_v_g': gain(ks[8], (L, C)),
        'gm_ws': nrm(ks[9], (L, GM_GROUPS, GM_CHUNK, GM_CHUNK), GM_CHUNK ** -0.5),
        'gm_b': 1.0 + 0.1 * jax.random.normal(ks[10], (L, GM_GROUPS, GM_CHUNK), f32),
        'pool_w': nrm(ks[11], (L, len(POOL_WINDOWS), POOL_GD, POOL_GD), POOL_GD ** -0.5),
        'pool_scale': gain(ks[12], (L, C)),
        'conv_dw': nrm(ks[13], (L, CONV_K_2, C), CONV_K_2 ** -0.5),
        'conv_b': nrm(ks[14], (L, C), 0.02),
        'conv_ln_g': gain(ks[15], (L, C)),
        'conv_ln_b': nrm(ks[16], (L, C), 0.02),
        'w_branch': nrm(ks[17], (L, N_BRANCH, C, D), C ** -0.5),
        'w_out': nrm(ks[18], (L, D, D), D ** -0.5),
        'ffn2_pre_g': gain(ks[19], (L, D)),
        'ffn2_post_g': gain(ks[20], (L, D)),
        'ffn2_w_gu': nrm(ks[21], (L, D, 2 * F), D ** -0.5),
        'ffn2_w_down': nrm(ks[22], (L, F, D), F ** -0.5),
        'rel_bias': nrm(ks[23], (REL_BUCKETS, ATT_HEADS), 0.5),
    }

def second_block(x, ffn1_pre_g, ffn1_post_g, ffn1_w_gu, ffn1_w_down, mix_pre_g, mix_post_g, w_in,
              gm_v_g, gm_ws, gm_b, pool_w, pool_scale, conv_dw, conv_b, conv_ln_g, conv_ln_b,
              w_branch, w_out, ffn2_pre_g, ffn2_post_g, ffn2_w_gu, ffn2_w_down, rel_bias):
    for l in range(DEPTH):
        h = swiglu_ffn(rmsnorm(x, ffn1_pre_g[l]), ffn1_w_gu[l], ffn1_w_down[l])
        x = x + 0.5 * rmsnorm(h, ffn1_post_g[l])
        h = mixing_sublayer(rmsnorm(x, mix_pre_g[l]), w_in[l], gm_v_g[l], gm_ws[l], gm_b[l],
                            pool_w[l], pool_scale[l], conv_dw[l], conv_b[l], conv_ln_g[l],
                            conv_ln_b[l], w_branch[l], w_out[l], rel_bias)
        x = x + rmsnorm(h, mix_post_g[l])
        h = swiglu_ffn(rmsnorm(x, ffn2_pre_g[l]), ffn2_w_gu[l], ffn2_w_down[l])
        x = x + 0.5 * rmsnorm(h, ffn2_post_g[l])
    return x


def setup_inputs(seed=0):
    out = dict(first_inputs(seed))
    for name, value in second_inputs(seed + 1).items():
        if name != "x":
            out[name + "_2"] = value
    return out


def reference(
    x, w_in, lower_bounds, hgrn_norm_w, conv_w, w_proj_hgrn, w_proj_conv, w_out, norm_mix,
    norm_ffn, dense_w1, dense_w3, dense_w2, router_w, expert_w1, expert_w3, expert_w2,
    final_norm, ffn1_pre_g_2, ffn1_post_g_2, ffn1_w_gu_2, ffn1_w_down_2, mix_pre_g_2,
    mix_post_g_2, w_in_2, gm_v_g_2, gm_ws_2, gm_b_2, pool_w_2, pool_scale_2, conv_dw_2,
    conv_b_2, conv_ln_g_2, conv_ln_b_2, w_branch_2, w_out_2, ffn2_pre_g_2, ffn2_post_g_2,
    ffn2_w_gu_2, ffn2_w_down_2, rel_bias_2,
):
    x = first_block(
        x, w_in, lower_bounds, hgrn_norm_w, conv_w, w_proj_hgrn, w_proj_conv, w_out, norm_mix,
        norm_ffn, dense_w1, dense_w3, dense_w2, router_w, expert_w1, expert_w3, expert_w2,
        final_norm,
    )
    return second_block(
        x, ffn1_pre_g_2, ffn1_post_g_2, ffn1_w_gu_2, ffn1_w_down_2, mix_pre_g_2, mix_post_g_2,
        w_in_2, gm_v_g_2, gm_ws_2, gm_b_2, pool_w_2, pool_scale_2, conv_dw_2, conv_b_2,
        conv_ln_g_2, conv_ln_b_2, w_branch_2, w_out_2, ffn2_pre_g_2, ffn2_post_g_2, ffn2_w_gu_2,
        ffn2_w_down_2, rel_bias_2,
    )


_drawn_inputs = setup_inputs


def setup_inputs(seed=0):
    import zlib

    import numpy as np

    out = dict(_drawn_inputs(seed))
    spreads = {}
    factors = {'lower_bounds': 2.685, 'gm_v_g_2': 3.052, 'conv_ln_b_2': 4.691, 'conv_b_2': 3.182}
    for name, (base, spread) in spreads.items():
        noise = np.random.default_rng([zlib.crc32(name.encode()), seed]).standard_normal(out[name].shape)
        drawn = base * np.exp(spread * noise) if base else spread * noise
        out[name] = __import__('jax').numpy.asarray(drawn.astype(out[name].dtype))
    for name, factor in factors.items():
        out[name] = (out[name] * factor).astype(out[name].dtype)
    return out
```

```python
from collections import defaultdict
from contextlib import ExitStack, contextmanager

import numpy as np

import concourse.bass as bass
from concourse import mybir

F32 = mybir.dt.float32
F32R = mybir.dt.float32r
U8 = mybir.dt.uint8
I32 = mybir.dt.int32
ALU = mybir.AluOpType
ACT = mybir.ActivationFunctionType
AX = mybir.AxisListType.X

P = 128
S = 256
NT = S // P
D = 1024
KT = D // P
FF = 2816
FT = FF // P
NE = 8
HEADS = 8
HGRN_SCALE = 128.0 ** -0.5
F_MIN = 1e-6
EPS = 1e-6
CW = 512
BIG = 3.0e38
BW = 256
REST = 164
TOPK = 64
REL_BUCKETS = 32

SLAB = 2048
RING = 3
WIN_GROUPS = 9 * D // CW
FF_GROUPS = 2 * FF // CW
FF_SLABS = 2 * FF_GROUPS + FT // 2
LEVELS = (1, 2, 4, 8, 16, 32, 64)

LEAD = 2
LCOLS = 41
PCOLS = 2 * LCOLS
PC2 = 98
MIX1_SLABS = 2 * WIN_GROUPS + 12
MIX2_SLABS = 24 + 1 + 4 + 4
N_SLABS = 2 * MIX1_SLABS + (1 + NE) * FF_SLABS + 2 * (2 * FF_SLABS + MIX2_SLABS)
MOE_BASE = 2 * MIX1_SLABS + FF_SLABS

CREDIT = 600


class Memo:

    def __init__(self):
        self.delta, self.event, self.last = {}, {}, False


class Core:

    SEM = {"pe": "s_pe", "act": "s_act", "dve": "s_dve", "pool": "s_pool", "sp": "s_sp"}

    def __init__(self, name, eng, sems, memo):
        self.name, self.eng, self.sems, self.memo = name, eng, sems, memo
        self.count = defaultdict(int)
        self.loops = []
        self.own = self.SEM[name]
        self.prefix, self.shift = "", 0
        self.pending = set()
        self.credits()

    def credits(self):
        for s in ("s_hi", "s_lo", "s_mm"):
            self.count[s] = RING
        for s in self.SEM.values():
            self.count[s] = CREDIT
        self.eng.sem_inc(self.s(self.own), CREDIT)
        ring = {"act": "s_hi", "dve": "s_lo", "pe": "s_mm"}.get(self.name)
        if ring:
            self.eng.sem_inc(self.s(ring), RING)

    def s(self, name):
        return self.sems(self.prefix + name)

    @contextmanager
    def aside(self, prefix, shift):
        kept = self.count, self.prefix, self.shift
        self.count, self.prefix, self.shift = defaultdict(int), prefix, shift
        self.credits()
        yield
        self.count, self.prefix, self.shift = kept

    @contextmanager
    def loop(self, name, trips):
        entry = dict(self.count)
        if self.loops:
            self.carry()
        with self.eng.Fori(0, trips) as reg:
            self.loops.append((name, reg, trips))
            yield reg
            self.loops.pop()
        delta = {s: v - entry.get(s, 0) for s, v in self.count.items() if v != entry.get(s, 0)}
        assert delta.get("slab", 0) % RING == 0
        self.memo.delta[self.name, name] = delta
        for s, d in delta.items():
            self.count[s] = entry.get(s, 0) + trips * d

    def value(self, s, plus=0):
        v = self.count[s] + plus
        for name, reg, _ in self.loops:
            d = self.memo.delta.get((self.name, name), {}).get(s, 0)
            if d:
                v = reg * d + v
        return v

    def do(self, ins, event=None, sem=None, n=1):
        s = sem or self.own
        ins.then_inc(self.s(s), n)
        self.pending = set()
        self.count[s] += n
        if event:
            self.note(event, s)
        return ins

    def note(self, event, s):
        self.memo.event[event] = (self.name, s, self.prefix, self.count[s], tuple(x[0] for x in self.loops), tuple(x[2] for x in self.loops))

    def wait(self, *events, back=0):
        for event in events:
            if self.memo.last:
                assert event in self.memo.event, event
            who, s, prefix, v, names, trips = self.memo.event.get(event, (self.name, self.own, self.prefix, CREDIT, (), ()))
            mine = {n: r for n, r, _ in self.loops}
            regs = []
            for i, (n, t) in enumerate(zip(names, trips)):
                d = self.memo.delta.get((who, n), {}).get(s, 0)
                if n in mine:
                    if i == len(names) - 1:
                        v -= back * d
                    if d:
                        regs.append((mine[n], d))
                else:
                    v += (t - 1) * d
            for r, d in regs:
                v = r * d + v
            self.wait_for(prefix + s, v)

    def wait_for(self, s, v):
        if self.loops and s in self.pending:
            self.carry()
        self.pending.add(s)
        self.eng.wait_ge(self.sems(s), v)

    def carry(self):
        self.eng.sem_inc(self.sems("s_carry"), 1)
        self.pending = set()

    def mark(self, event):
        self.note(event, self.own)

    def sync(self):
        self.wait_for(self.prefix + self.own, self.value(self.own))

    def dma(self, out, in_, event, **kw):
        s = "d_" + event
        if self.loops:
            self.carry()
        self.do(self.eng.dma_start(out, in_, **kw), event, s, 16)


class Kernel:

    def __init__(self, nc, args, out, memo, stop=None):
        self.nc, self.a, self.out, self.memo, self.stop = nc, args, out, memo, stop
        self.stack = ExitStack()
        self.semtab = {}

    def sem(self, name):
        if name not in self.semtab:
            self.semtab[name] = self.stack.enter_context(self.nc.semaphore(name))
        return self.semtab[name]

    def sb(self, name, shape, dt=F32, stack=None):
        return (stack or self.stack).enter_context(self.nc.sbuf_tensor(name, shape, dt))

    def overlays(self, name, size, *variants):
        made = {}
        for variant in variants:
            with ExitStack() as st:
                for n, shape, dt in variant:
                    made[n] = self.sb(n, shape, dt, st)
        self.sb(name, [P, size])
        return made

    def memory(self):
        self.raw = self.sb("raw", [P, RING, SLAB])
        self.whi = self.sb("whi", [P, RING, SLAB], F32R)
        self.wlo = self.sb("wlo", [P, RING, SLAB], F32R)
        self.X = self.sb("X", [P, NT, D])
        self.XN = self.sb("XN", [P, NT, D])
        self.XH = self.sb("XH", [P, KT, S], F32R)
        self.XL = self.sb("XL", [P, KT, S], F32R)
        self.ident = self.sb("ident", [P, P])
        self.small = self.sb("small", [P, 192])
        self.pcols = self.sb("pcols", [P, PCOLS])
        b = self.overlays("region_b", 6816, [
            ("mcum", [P, 12 * P], F32R),
            ("masks", [P, 7, P], U8),
            ("E1", [P, NT, 8, P], F32),
            ("KQ", [P, 2, 2 * S], F32),
            ("LFH", [P, 2, NT, P], F32R), ("LFL", [P, 2, NT, P], F32R),
            ("SM", [P, 2, NT, P], F32), ("SC", [P, 2, P], F32),
        ], [
            ("mcum_f", [P, 12 * P], F32), ("masks_", [P, 7, P], U8), ("mload", [P, 12 * P], F32), ("mask_load", [P, 7, P], F32),
        ], [
            ("RB", [P, NT, 4, S], F32),
            ("MP", [P, 4, 3 * P], F32),
            ("WS", [P, 4, P], F32),
            ("PW", [P, 4, 64], F32),
            ("pc2", [P, PC2], F32),
            ("gvb", [P, BW], F32),
            ("ones", [P, P], F32),
        ])
        self.mcum, self.masks, self.E1, self.KQ, self.LFH, self.LFL, self.SM = (b[n] for n in ("mcum", "masks", "E1", "KQ", "LFH", "LFL", "SM",))
        self.SC, self.mload, self.RB, self.MP, self.WS, self.PW, self.pc2 = (b[n] for n in ("SC", "mload", "RB", "MP", "WS", "PW", "pc2",))
        self.gvb, self.ones, self.mask_load = (b[n] for n in ("gvb", "ones", "mask_load"))
        n = WIN_GROUPS * NT * CW
        z = self.overlays("region_z", n, [("Z", [P, n], F32)], [
            ("GH", [P, FT, S], F32R), ("GL", [P, FT, S], F32R),
            ("SG", [P, 3, NT, S], F32), ("GN", [P, 3, NT, S], F32),
        ], [
            ("GH_", [P, FT, P], F32R), ("GL_", [P, FT, P], F32R),
            ("SG_", [P, 3, S], F32), ("GN_", [P, 3, S], F32),
            ("XEH", [P, KT, P], F32R), ("XEL", [P, KT, P], F32R),
            ("PM", [P, NT, P], F32),
            ("PT", [P, S], F32R),
            ("YH", [P, D], F32R), ("YL", [P, D], F32R),
            ("GB", [P, D], F32), ("RW", [P, KT, NE], F32), ("RWH", [P, KT, NE], F32R), ("RWL", [P, KT, NE], F32R),
            ("iota_", [P, P], F32), ("iota", [P, P], F32), ("ltri", [P, 3, P], F32), ("mo", [P, 512], F32),
        ], [
            ("Z2", [P, 12 * NT * CW], F32),
            ("HP", [P, 2, 30 + S], F32), ("CA", [P, 2, S], F32), ("CB", [P, 2, S], F32),
            ("QT", [P, 2, S], F32), ("KTT", [P, 2, S], F32), ("QI", [P, 2, S], F32),
            ("LG", [P, 4, S], F32), ("SCO", [P, 2, S], F32), ("WRK", [P, 2, S], F32), ("m8", [P, 16], F32),
        ], [("GP", [P, D], F32), ("TMPG", [P, 56 * S], F32)])
        self.Z, self.GH, self.GL, self.SG, self.GN, self.GH_, self.GL_ = (z[n] for n in ("Z", "GH", "GL", "SG", "GN", "GH_", "GL_",))
        self.SG_, self.GN_, self.XEH, self.XEL, self.PM, self.PT, self.YH = (z[n] for n in ("SG_", "GN_", "XEH", "XEL", "PM", "PT", "YH",))
        self.YL, self.GB, self.RW, self.RWH, self.RWL, self.iota_, self.iota = (z[n] for n in ("YL", "GB", "RW", "RWH", "RWL", "iota_", "iota",))
        self.ltri, self.mo, self.Z2, self.HP, self.CA, self.CB, self.QT = (z[n] for n in ("ltri", "mo", "Z2", "HP", "CA", "CB", "QT",))
        self.KTT, self.QI, self.LG, self.SCO, self.WRK, self.m8, self.GP = (z[n] for n in ("KTT", "QI", "LG", "SCO", "WRK", "m8", "GP",))
        self.TMPG = z["TMPG"]
        self.ps = self.stack.enter_context(self.nc.psum_tensor("ps", [P, 8, CW], F32))

    def eps(self):
        return self.small[:, 0:1]

    def load_slab(self, k):
        slot = k.count["slab"] % RING
        k.eng.wait_ge(k.s("s_lo"), k.value("slab", 1))
        src = self.a["W"][bass.ds(k.value("slab", k.shift), 1), :, :].rearrange("a p n -> p (a n)")
        k.eng.dma_start(self.raw[:, slot, :], src).then_inc(k.s(f"s_land{slot}"), 16)
        k.count["slab"] += 1

    def hi_slab(self, k):
        slot = k.count["slab"] % RING
        k.count[f"land{slot}"] += 16
        k.eng.wait_ge(k.s(f"s_land{slot}"), k.value(f"land{slot}"))
        k.eng.wait_ge(k.s("s_mm"), k.value("slab", 1))
        k.do(k.eng.activation(self.whi[:, slot, :], self.raw[:, slot, :], ACT.Copy), sem="s_hi")
        k.count["slab"] += 1

    def lo_slab(self, k):
        slot = k.count["slab"] % RING
        k.eng.wait_ge(k.s("s_hi"), k.value("slab", 1 + RING))
        k.do(k.eng.tensor_tensor(self.wlo[:, slot, :], self.raw[:, slot, :], self.whi[:, slot, :], ALU.subtract), sem="s_lo")
        k.count["slab"] += 1

    def feed(self, k, n):
        part = {"sp": self.load_slab, "act": self.hi_slab, "dve": self.lo_slab}.get(k.name)
        if part:
            for _ in range(n):
                part(k)

    def mm_slab(self, k, terms, event=None):
        slot = k.count["slab"] % RING
        k.eng.wait_ge(k.s("s_lo"), k.value("slab", 1 + RING))
        for ps, xh, xl, cols, first, last in terms:
            wh, wl = self.whi[:, slot, cols], self.wlo[:, slot, cols]
            k.eng.matmul(ps, xh, wh, start=first, stop=False)
            k.eng.matmul(ps, xh, wl, start=False, stop=False)
            mm = k.eng.matmul(ps, xl, wh, start=False, stop=last)
        k.do(mm, event, sem="s_mm")
        k.count["slab"] += 1

    def column_terms(self, half, bank, XH, XL, tiles=NT):
        return [(self.ps[:, bank + t, :], XH[:, 4 * half + c, t * P:(t + 1) * P], XL[:, 4 * half + c, t * P:(t + 1) * P],
                 slice(c * CW, (c + 1) * CW), half == 0 and c == 0, half == 1 and c == 3)
                for t in range(tiles) for c in range(4)]

    def row_terms(self, j, n, GH, GL, banks):
        return [(self.ps[:, banks[t][h], :], GH[:, 2 * j + c, t * P:(t + 1) * P], GL[:, 2 * j + c, t * P:(t + 1) * P],
                 slice(c * D + h * CW, c * D + (h + 1) * CW), j == 0 and c == 0, j == n - 1 and c == 1)
                for t in range(len(banks)) for c in range(2) for h in range(2)]

    def groups(self, k, tag, n, evac, ready=(), per=3):
        def body(g, j, looped):
            pair = 2 * (j % 3)
            self.feed(k, 2)
            if k.name == "pe":
                if looped:
                    k.wait(f"{tag}.ev{j}", back=1)
                self.mm_slab(k, self.column_terms(0, pair, self.XH, self.XL))
                self.mm_slab(k, self.column_terms(1, pair, self.XH, self.XL), event=f"{tag}.mm{j}")
            evac(k, g, j, pair)

        assert n % per == 0
        if k.name == "pe":
            k.wait(*ready)
        if n > per:
            with k.loop(tag, n // per) as it:
                for j in range(per):
                    body(it * per + j, j, True)
        else:
            for j in range(per):
                body(j, j, False)

    def start(self, k):
        if k.name == "pool":
            k.do(k.eng.memset(self.ident[:], 0.0)); k.sync()
            k.do(k.eng.affine_select(out=self.ident[:], in_=self.ident[:], compare_op=ALU.not_equal, fill=1.0, base=0,
                                     pattern=[[-1, P]], channel_multiplier=1), "ident")
        if k.name == "dve":
            k.do(k.eng.memset(self.eps(), EPS), "eps")
        if k.name == "pool":
            k.dma(self.X[:], self.a["x"].rearrange("(t p) d -> p t d", p=P), "x")
            k.dma(self.pcols[:], self.a["pcols"], "pcols")
            k.dma(self.mload[:], self.a["cum_sums"], "mload")
            k.dma(self.mask_load[:], self.a["level_masks"], "mask_load")
        self.feed(k, LEAD)
        if k.name == "dve":
            k.wait("mload")
            k.do(k.eng.tensor_copy(self.mcum[:], self.mload[:]), "mcum")
            k.wait("mask_load")
            k.do(k.eng.tensor_copy(self.masks[:], self.mask_load[:]), "masks")

    def rstd(self, k, tag, src, ready, junk, n=NT, width=D):
        ss, rs = self.small[:, 8:8 + n], self.small[:, 16:16 + n]
        if k.name == "act":
            k.wait(*ready)
            for i in range(n):
                k.do(k.eng.activation(junk(i), src(i), ACT.Square, accum_out=ss[:, i:i + 1]))
            k.sync()
            k.do(k.eng.activation(rs, ss, ACT.Sqrt, scale=1.0 / width, bias=self.eps()), f"{tag}.rms")
        if k.name == "dve":
            k.wait(f"{tag}.rms")
            k.do(k.eng.reciprocal(rs, rs), f"{tag}.rstd")
        return rs

    def norm_in(self, k, tag, ready, gain):
        rs = self.rstd(k, tag, lambda i: self.X[:, i, :], ready, lambda i: self.XN[:, i, :])
        if k.name == "dve":
            k.sync()
            for t in range(NT):
                k.do(k.eng.tensor_scalar(self.XN[:, t, :], self.X[:, t, :], rs[:, t:t + 1], None, ALU.mult), f"{tag}.xn")
        self.transposed(k, tag, [f"{tag}.xn"], lambda i, t: self.XN[:, t, i * P:(i + 1) * P], gain)

    def split_into(self, k, tag, ready, *parts):
        if k.name == "act":
            k.wait(*ready)
            for ps, H, L, gain in parts:
                k.do(k.eng.activation(H, ps, ACT.Copy, **({} if gain is None else {"scale": gain})), f"{tag}.h")
        if k.name == "dve":
            k.wait(f"{tag}.h")
            for ps, H, L, gain in parts:
                if gain is None:
                    k.do(k.eng.tensor_tensor(L, ps, H, ALU.subtract), f"{tag}.l")
                else:
                    k.do(k.eng.scalar_tensor_tensor(out=L, in0=ps, scalar=gain, in1=H, op0=ALU.mult, op1=ALU.subtract), f"{tag}.l")

    def transposed(self, k, tag, ready, src, gain, n=KT, at=0, bank0=0):
        if k.name == "pe":
            k.wait(*ready)
        for b in range(n // 2):
            bank = self.ps[:, bank0 + b, :]
            if k.name == "pe":
                for i in range(2):
                    for t in range(NT):
                        mm = k.eng.transpose(bank[:, i * S + t * P:i * S + (t + 1) * P], src(2 * b + i, t), self.ident[:])
                k.do(mm, f"{tag}.tp{b}")
            j = at + 2 * b
            if gain is None:
                parts = [(bank.rearrange("p (a b) -> p a b", a=2), self.XH[:, j:j + 2, :], self.XL[:, j:j + 2, :], None)]
            else:
                parts = [(bank[:, i * S:(i + 1) * S], self.XH[:, j + i, :], self.XL[:, j + i, :], gain(2 * b + i)) for i in range(2)]
            self.split_into(k, f"{tag}{b}", [f"{tag}.tp{b}"], *parts)
        if k.name == "dve":
            k.mark(f"{tag}.split")

    def zview(self, s, Z=None):
        return (Z or self.Z)[:, s * NT * D:(s + 1) * NT * D].rearrange("p (g t c) -> p g t c", g=2, t=NT)

    def mixer1(self, k, l):
        T = f"m{l}."
        c0 = l * LCOLS
        pc = self.pcols
        f, v, q, gout, cb, cc, cu, ga, gb = range(9)
        seg = self.zview
        self.norm_in(k, T + "n", ["x", "pcols", "eps", "ident"] if l == 0 else [f"f{l - 1}.out"], lambda i: pc[:, c0 + i:c0 + i + 1])
        LB = self.XN
        TMP = self.E1[:].rearrange("p a b c -> p (a b c)").rearrange("p (a b) -> p a b", a=2)
        if k.name == "pool":
            k.wait(T + "n.split")
            k.dma(LB[:], self.a["lower_bounds"].rearrange("(o l) d -> o l d", o=1).broadcast_to([P, 2, D]), T + "lb")
        if k.name == "dve":
            k.wait(T + "lb", "masks")
            k.do(k.eng.tensor_tensor(TMP[:, 0, :], LB[:, 0, :], LB[:, 1, :], ALU.max)); k.sync()
            for i in range(2):
                k.do(k.eng.tensor_tensor(LB[:, i, :], LB[:, i, :], TMP[:, 0, :], ALU.subtract), T + "lbe")
        if k.name == "act":
            k.wait(T + "lbe")
            k.do(k.eng.activation(LB[:], LB[:], ACT.Exp), T + "lbx")
        if k.name == "dve":
            k.wait(T + "lbx")
            k.do(k.eng.tensor_tensor(TMP[:, 0, :], LB[:, 0, :], LB[:, 1, :], ALU.add)); k.sync()
            k.do(k.eng.reciprocal(TMP[:, 1, :], TMP[:, 0, :])); k.sync()
            for i in range(2):
                k.do(k.eng.tensor_tensor(LB[:, i, :], LB[:, i, :], TMP[:, 1, :], ALU.mult))
            k.sync()
            if l == 1:
                k.do(k.eng.tensor_tensor(LB[:, 1, :], LB[:, 0, :], LB[:, 1, :], ALU.add)); k.sync()
                k.do(k.eng.tensor_tensor(LB[:, 1, :], LB[:, 1, :], LB[:, 0, :], ALU.subtract)); k.sync()
            else:
                k.do(k.eng.tensor_tensor(LB[:, 1, :], LB[:, 0, :], LB[:, 0, :], ALU.subtract)); k.sync()
            k.do(k.eng.tensor_scalar(LB[:, 0, :], LB[:, 1, :], -1.0, 1.0, ALU.mult, ALU.add), T + "lbd")

        def evac(k, g, j, pair):
            if k.name == "act":
                k.wait(T + f"w.mm{j}")
                k.do(k.eng.activation(self.Z[:, bass.ds(g * (NT * CW), NT * CW)],
                                      self.ps[:, pair:pair + 2, :].rearrange("p a b -> p (a b)"), ACT.Copy), T + f"w.ev{j}")
        self.groups(k, T + "w", WIN_GROUPS, evac, ready=[T + "n.split"])
        if k.name == "act":
            k.mark(T + "w.done")

        lbv = lambda i, g: LB[:, i, g * CW:(g + 1) * CW].rearrange("p (o c) -> p o c", o=1).broadcast_to([P, NT, CW])
        KN = seg(cu)
        if k.name == "dve":
            k.wait(T + "w.done")
            k.do(k.eng.tensor_tensor(seg(cb), seg(cb), seg(cu), ALU.mult), T + "bu")
        if k.name == "act":
            k.sync()
            k.wait(T + "bu", T + "lbd")
            k.do(k.eng.activation(KN, seg(f), ACT.Sigmoid, scale=-1.0), T + "kn0")
            k.sync()
            k.do(k.eng.activation(seg(f), seg(f), ACT.Sigmoid), T + "f0")
            k.do(k.eng.activation(seg(ga), seg(ga), ACT.Sigmoid))
            k.do(k.eng.activation(seg(gb), seg(gb), ACT.Sigmoid), T + "gates")
            k.do(k.eng.activation(seg(q), seg(q), ACT.Silu), T + "q")
            k.do(k.eng.activation(seg(gout), seg(gout), ACT.Silu), T + "g")
            k.wait(T + "f3")
            k.do(k.eng.activation(seg(f), seg(f), ACT.Ln), T + "logf")
        if k.name == "dve":
            k.wait(T + "kn0")
            for g in range(2):
                k.do(k.eng.tensor_tensor(KN[:, g], KN[:, g], lbv(0, g), ALU.mult), T + "kn")
            k.wait(T + "f0")
            for i, op in ((0, ALU.mult), (1, ALU.add)):
                for g in range(2):
                    k.do(k.eng.tensor_tensor(seg(f)[:, g], seg(f)[:, g], lbv(i, g), op))
                k.sync()
            k.do(k.eng.tensor_scalar(seg(f), seg(f), F_MIN, None, ALU.max), T + "f3")

        self.hgrn(k, T)
        O = seg(v)
        O3 = self.Z[:, v * NT * D:(v + 1) * NT * D].rearrange("p (n c) -> p n c", c=P)
        SQ = self.XN[:].rearrange("p t d -> p (t d)").rearrange("p (n c) -> p n c", c=P)
        ss, rs = self.small[:, 32:48], self.small[:, 48:64]
        if k.name == "dve":
            k.wait(T + "h.done", T + "g")
            k.do(k.eng.tensor_tensor(SQ, O3, O3, ALU.mult)); k.sync()
            k.do(k.eng.tensor_reduce(ss, SQ, AX, ALU.add), T + "oss")
            k.do(k.eng.tensor_tensor(O, O, seg(gout), ALU.mult))
        if k.name == "act":
            k.wait(T + "oss")
            k.do(k.eng.activation(rs, ss, ACT.Sqrt, scale=1.0 / P, bias=self.eps()), T + "orms")
        if k.name == "dve":
            k.wait(T + "orms")
            k.do(k.eng.reciprocal(rs, rs)); k.sync()
            k.do(k.eng.tensor_tensor(O3, O3, rs.rearrange("p (n o) -> p n o", o=1).broadcast_to([P, 16, P]), ALU.mult), T + "on")
        gw = pc[:, c0 + 16:c0 + 17]
        self.transposed(k, T + "o", [T + "on"], lambda i, t: O[:, i // 4, t, (i % 4) * P:(i % 4 + 1) * P], lambda i: gw)

        YA, YB = seg(q), seg(f)
        def evac_a(k, g, j, pair):
            if k.name == "dve":
                k.wait(T + f"a.mm{j}", T + "gates")
                k.do(k.eng.tensor_tensor(YA[:, j], self.ps[:, pair:pair + 2, :], seg(ga)[:, j], ALU.mult), T + f"a.ev{j}")
        self.groups(k, T + "a", 2, evac_a, per=2, ready=[T + "o.split"])

        CV = self.XN[:].rearrange("p t d -> p (t d)").rearrange("p (n c) -> p n c", c=S)
        w = lambda j, i: pc[:, c0 + 17 + 8 * j + i:c0 + 18 + 8 * j + i]
        for i in range(KT):
            bank = self.ps[:, 4 + i % 4, :]
            tag = T + f"c{i}"
            if k.name == "pe":
                if i == 0:
                    k.wait(T + "a.ev1")
                if i >= 4:
                    k.wait(T + f"c{i - 4}.y")
                for a, s in enumerate((cb, cc)):
                    for t in range(NT):
                        mm = k.eng.transpose(bank[:, a * S + t * P:a * S + (t + 1) * P], seg(s)[:, i // 4, t, (i % 4) * P:(i % 4 + 1) * P], self.ident[:])
                k.do(mm, tag + ".tp")
            if k.name == "dve":
                k.wait(tag + ".tp")
                k.do(k.eng.tensor_scalar(CV[:, i, :], bank[:, 0:S], w(2, i), None, ALU.mult)); k.sync()
                for j in (1, 2):
                    k.do(k.eng.scalar_tensor_tensor(out=CV[:, i, j:], in0=bank[:, 0:S - j], scalar=w(2 - j, i), in1=CV[:, i, j:], op0=ALU.mult, op1=ALU.add)); k.sync()
                k.do(k.eng.tensor_tensor(CV[:, i, :], CV[:, i, :], bank[:, S:], ALU.mult), tag + ".y")
        for i in range(0, KT, 2):
            if k.name == "act":
                k.wait(T + f"c{i + 1}.y", T + "a.mm1")
                k.do(k.eng.activation(self.XH[:, i:i + 2, :], CV[:, i:i + 2, :], ACT.Copy), T + f"cv{i}")
            if k.name == "dve":
                k.wait(T + f"cv{i}")
                k.do(k.eng.tensor_tensor(self.XL[:, i:i + 2, :], CV[:, i:i + 2, :], self.XH[:, i:i + 2, :], ALU.subtract), T + "cv.split")

        def evac_b(k, g, j, pair):
            if k.name == "dve":
                k.wait(T + f"b.mm{j}")
                k.do(k.eng.tensor_tensor(YB[:, j], self.ps[:, pair:pair + 2, :], seg(gb)[:, j], ALU.mult), T + f"b.ev{j}")
                k.sync()
                k.do(k.eng.tensor_tensor(YA[:, j], YA[:, j], YB[:, j], ALU.add), T + "merged")
        self.groups(k, T + "b", 2, evac_b, per=2, ready=[T + "cv.split"])
        self.transposed(k, T + "y", [T + "merged"], lambda i, t: YA[:, i // 4, t, (i % 4) * P:(i % 4 + 1) * P], None)
        def evac_o(k, g, j, pair):
            if k.name == "dve":
                k.wait(T + f"w2.mm{j}")
                xs = self.X[:, :, j * CW:(j + 1) * CW]
                k.do(k.eng.tensor_tensor(xs, self.ps[:, pair:pair + 2, :], xs, ALU.add), T + f"w2.ev{j}")
        self.groups(k, T + "w2", 2, evac_o, per=2, ready=[T + "y.split"])
        if k.name == "dve":
            k.mark(T + "out")

    def hgrn(self, k, T):
        f, v, q, KSEG = 0, 1, 2, 6
        ps, LFH, LFL, KQ, SM, SC = self.ps, self.LFH, self.LFL, self.KQ, self.SM, self.SC
        EB = [self.XN[:].rearrange("p t (l c) -> p t l c", l=8), self.E1[:]]
        stage = lambda b, i: EB[b][:, 0, 2 * i:2 * i + 2, :]
        U = T + "h"
        if k.name == "pe":
            k.wait(T + "w.done", "mcum")
        if k.name == "dve":
            k.wait("masks")
        with k.loop(U, HEADS // 2) as it:
            def head(seg, b):
                off = it * (2 * P) + (it // 2) * CW + (seg * NT * D + b * P)
                return self.Z[:, bass.ds(off, CW + P)].rearrange("p (a c) -> p a c", c=P)[:, 0:5:4, :]
            ev = lambda n, b: f"{U}.{n}{b}"
            for b in range(2):
                B, e = 4 * b, (lambda n, b=b: ev(n, b))
                if k.name == "act":
                    k.wait(T + "kn", T + "logf")
                    k.wait(e("cum"), back=1)
                    k.do(k.eng.activation(LFH[:, b], head(f, b), ACT.Copy), e("lfh"))
                    k.wait(e("sc2"), back=1)
                    k.do(k.eng.activation(stage(b, 0), head(KSEG, b), ACT.Copy))
                    k.do(k.eng.activation(stage(b, 1), head(q, b), ACT.Copy, scale=HGRN_SCALE), e("qs"))
                if k.name == "dve":
                    k.wait(e("lfh"))
                    k.do(k.eng.tensor_tensor(LFL[:, b], head(f, b), LFH[:, b], ALU.subtract), e("lfl"))
                if k.name == "pe":
                    k.wait(e("qs"))
                    k.wait(e("o"), back=1)
                    for i in range(2):
                        for t in range(NT):
                            mm = k.eng.transpose(ps[:, B, i * S + t * P:i * S + (t + 1) * P], stage(b, i)[:, t, :], self.ident[:])
                    k.do(mm, e("tq"))
                if k.name == "act":
                    k.wait(e("tq"))
                    k.do(k.eng.activation(KQ[:, b], ps[:, B, :], ACT.Copy), e("kq"))
                if k.name == "pe":
                    k.wait(e("kq"), e("lfl"))
                    for t in range(NT):
                        for half in range(2):
                            c = half + (half and t)
                            cols = self.mcum[:, c * CW:(c + 1) * CW]
                            k.eng.matmul(ps[:, B + 2 * t + half, :], LFH[:, b, t, :], cols, start=True, stop=False)
                            mm = k.eng.matmul(ps[:, B + 2 * t + half, :], LFL[:, b, t, :], cols, start=False, stop=True)
                    k.do(mm, e("cum"))
                if k.name == "act":
                    k.wait(e("cum"))
                    for t in range(NT):
                        for half in range(2):
                            k.do(k.eng.activation(EB[b][:, t, 4 * half:4 * half + 4, :], ps[:, B + 2 * t + half, :].rearrange("p (l c) -> p l c", l=4), ACT.Exp), e("exp"))
                if k.name == "dve":
                    k.wait(e("exp"))
                    for i, m in enumerate(LEVELS):
                        for half in range(2):
                            for t in range(NT) if m < 64 else (None,):
                                if t is None:
                                    x = EB[b][:, :, i, half * m:half * m + m]
                                    y = KQ[:, b, half * S:(half + 1) * S].rearrange("p (t c) -> p t c", t=NT)[:, :, half * m:half * m + m]
                                else:
                                    x = EB[b][:, t, i, :].rearrange("p (n h m) -> p n h m", h=2, m=m)[:, :, half, :]
                                    y = KQ[:, b, half * S + t * P:half * S + (t + 1) * P].rearrange("p (n h m) -> p n h m", h=2, m=m)[:, :, half, :]
                                k.do(k.eng.tensor_tensor(x, x, y, ALU.mult))
                    for t in range(NT):
                        x = EB[b][:, t, 7, :]
                        k.do(k.eng.tensor_tensor(x, x, KQ[:, b, t * S + t * P:t * S + (t + 1) * P], ALU.mult), e("x"))
            for b in range(2):
                B, e = 4 * b, (lambda n, b=b: ev(n, b))
                if k.name == "pe":
                    k.wait(e("x"))
                    for n in range(8):
                        for t in range(NT):
                            o = ps[:, B + n // 2, (n % 2) * S + t * P:(n % 2) * S + (t + 1) * P]
                            x = EB[b][:, t, n, :]
                            if n < 7:
                                mm = k.eng.matmul(o, x, x, start=True, stop=True)
                            else:
                                mm = k.eng.matmul(o, KQ[:, b, t * P:(t + 1) * P], KQ[:, b, S + t * P:S + (t + 1) * P], start=True, stop=True)
                    k.do(mm, e("sc"))
                if k.name == "dve":
                    k.wait(e("sc"))
                    k.wait(e("av"), back=1)
                    slot = lambda n: ps[:, B + n // 2, (n % 2) * S:(n % 2 + 1) * S].rearrange("p (t c) -> p t c", t=NT)
                    one = lambda m: m.rearrange("p (o c) -> p o c", o=1).broadcast_to([P, NT, P])
                    k.do(k.eng.tensor_tensor(SM[:, b], slot(7), one(self.ident[:]), ALU.mult))
                    for n in range(7):
                        k.sync()
                        k.carry()
                        k.do(k.eng.copy_predicated(SM[:, b], one(self.masks[:, n, :]), slot(n)), e("sm"))
            for b in range(2):
                B, e = 4 * b, (lambda n, b=b: ev(n, b))
                if k.name == "pe":
                    k.wait(e("sm"))
                    k.do(k.eng.matmul(ps[:, B, 0:P], EB[b][:, 0, 7, :], EB[b][:, 1, 7, :], start=True, stop=True), e("sc2"))
                if k.name == "act":
                    k.wait(e("sc2"))
                    k.wait(e("av"), back=1)
                    k.do(k.eng.activation(SC[:, b], ps[:, B, 0:P], ACT.Copy), e("sx"))
                if k.name == "pe":
                    k.wait(e("sx"))
                    vv = head(v, b)
                    k.eng.matmul(ps[:, B + 1, 0:P], SM[:, b, 0, :], vv[:, 0, :], start=True, stop=True)
                    k.eng.matmul(ps[:, B + 1, P:2 * P], SM[:, b, 1, :], vv[:, 1, :], start=True, stop=False)
                    k.do(k.eng.matmul(ps[:, B + 1, P:2 * P], SC[:, b], vv[:, 0, :], start=False, stop=True), e("av"))
                if k.name == "act":
                    k.wait(e("av"))
                    k.do(k.eng.activation(head(v, b), ps[:, B + 1, 0:2 * P].rearrange("p (t c) -> p t c", t=NT), ACT.Copy), e("o"))
        if k.name == "act":
            k.mark(T + "h.done")

    def ff(self, k, T, tiles, ready, after_first=None, in_down=None):
        if tiles == NT:
            XH, XL, GH, GL, SG, GN = self.XH, self.XL, self.GH, self.GL, self.SG, self.GN
            bank, tpb, down = (lambda r: 2 * r), 6, ((0, 1), (4, 5))
            sg = lambda T_, r: T_[:, r]
            turned = self.ps[:, 6:8, 0:S]
        else:
            XH, XL, GH, GL, SG, GN = self.XEH, self.XEL, self.GH_, self.GL_, self.SG_, self.GN_
            bank, tpb, down = (lambda r: r), 3, ((4, 5),)
            sg = lambda T_, r: T_[:, r:r + 1]
            turned = self.ps[:, 3, 0:S].rearrange("p (a b) -> p a b", a=2)

        def products(n, r, freed, back=0):
            self.feed(k, 2)
            if k.name == "pe":
                if freed:
                    k.wait(f"{T}.gn{freed}", back=back)
                self.mm_slab(k, self.column_terms(0, bank(r), XH, XL, tiles))
                self.mm_slab(k, self.column_terms(1, bank(r), XH, XL, tiles), event=f"{T}.mm{n}")

        def gate(n, r):
            src = self.ps[:, bank(r):bank(r) + tiles, :]
            if k.name == "act":
                k.wait(f"{T}.mm{n}")
                k.do(k.eng.activation(sg(SG, r), src[:, :, 0:S], ACT.Silu), f"{T}.sg{n}")
            if k.name == "dve":
                k.wait(f"{T}.sg{n}")
                k.do(k.eng.tensor_tensor(sg(GN, r), sg(SG, r), src[:, :, S:], ALU.mult), f"{T}.gn{n}")

        def turn(n, r, at, prev, back=0, pback=0):
            if k.name == "pe":
                k.wait(f"{T}.gn{n}", back=back)
                if prev:
                    k.wait(f"{T}.gl{prev}", back=pback)
                for fb in range(2):
                    for t in range(tiles):
                        mm = k.eng.transpose(turned[:, fb, t * P:(t + 1) * P], sg(GN, r)[:, t, fb * P:(fb + 1) * P], self.ident[:])
                k.do(mm, f"{T}.tp{n}t")
            to = lambda G: G[:, bass.ds(at * 2, 2), :]
            if k.name == "act":
                k.wait(f"{T}.tp{n}t")
                k.do(k.eng.activation(to(GH), turned, ACT.Copy), f"{T}.gh{n}t")
            if k.name == "dve":
                k.wait(f"{T}.gh{n}t")
                k.do(k.eng.tensor_tensor(to(GL), turned, to(GH), ALU.subtract), f"{T}.gl{n}t")

        if k.name == "pe":
            k.wait(*ready)
        products("P", 0, None)
        gate("P", 0)
        if after_first:
            after_first()
        with k.loop(T + ".up", 3) as it:
            for j in range(3):
                r, before = (j + 1) % 3, (j + 2) % 3
                products(f"L{j}", r, f"L{j}", back=1)
                turn_name = f"L{before}"
                if k.name == "pe":
                    k.wait(f"{T}.gn{turn_name}", back=1 if j == 0 else 0)
                    k.wait(f"{T}.gl{(j + 2) % 3}s", back=1 if j == 0 else 0)
                    for fb in range(2):
                        for t in range(tiles):
                            mm = k.eng.transpose(turned[:, fb, t * P:(t + 1) * P], sg(GN, j)[:, t, fb * P:(fb + 1) * P], self.ident[:])
                    k.do(mm, f"{T}.tp{j}s")
                to = lambda G: G[:, bass.ds(it * 6 + 2 * j, 2), :]
                if k.name == "act":
                    k.wait(f"{T}.tp{j}s")
                    k.do(k.eng.activation(to(GH), turned, ACT.Copy), f"{T}.gh{j}s")
                if k.name == "dve":
                    k.wait(f"{T}.gh{j}s")
                    k.do(k.eng.tensor_tensor(to(GL), turned, to(GH), ALU.subtract), f"{T}.gl{j}s")
                gate(f"L{j}", r)
        products("E", 1, "L0")
        if k.name == "pe":
            k.wait(f"{T}.gl2s")
        turn("L2", 0, 9, None)
        gate("E", 1)
        n = FT // 2
        for j in range(n):
            self.feed(k, 1)
            if k.name == "pe":
                if j == 1:
                    k.wait(f"{T}.glEt")
                self.mm_slab(k, self.row_terms(j if j < n else j, n, GH, GL, down), event=f"{T}.down")
            if j == 0:
                turn("E", 1, 10, "L2t")
            if in_down and j == 4:
                in_down()
        return down

    def ffn1(self, k):
        self.norm_in(k, "f0n", ["m0.out"], lambda i: self.pcols[:, 8 + i:9 + i])
        self.ff(k, "f0", NT, ["f0n.split"])
        if k.name == "dve":
            k.wait("f0.down")
            for t in range(NT):
                k.do(k.eng.tensor_tensor(self.X[:, t, :], self.ps[:, 4 * t:4 * t + 2, :].rearrange("p a b -> p (a b)"), self.X[:, t, :], ALU.add))
            k.mark("f0.out")

    def moe(self, k):
        T, sm = "e.", self.small
        rs = self.rstd(k, T + "n", lambda i: self.X[:, i, :], ["m1.out"], lambda i: self.XN[:, i, :])
        if k.name == "pool":
            k.wait("m1.out")
            k.dma(self.GB[:], self.a["norm_ffn"][1:2, :].broadcast_to([P, D]), T + "gb")
            k.dma(self.RW[:], self.a["router_w"].rearrange("o (k p) e -> p (o k) e", p=P), T + "rw")
            k.do(k.eng.iota(self.iota_[:].bitcast(I32), pattern=[[1, P]], base=0, channel_multiplier=0), T + "iota_")
            k.do(k.eng.memset(self.ltri[:, 1:3, :], 1.0)); k.sync()
            k.do(k.eng.affine_select(out=self.ltri[:, 0, :], in_=self.ltri[:, 1, :], compare_op=ALU.is_gt, fill=0.0, base=0,
                                     pattern=[[1, P]], channel_multiplier=-1), T + "ltri")
        if k.name == "dve":
            k.sync()
            for t in range(NT):
                k.do(k.eng.tensor_scalar(self.XN[:, t, :], self.X[:, t, :], rs[:, t:t + 1], None, ALU.mult))
            k.sync(); k.wait(T + "gb")
            for t in range(NT):
                k.do(k.eng.tensor_tensor(self.XN[:, t, :], self.XN[:, t, :], self.GB[:], ALU.mult), T + "xn")
            k.wait(T + "iota_", T + "rw")
            k.do(k.eng.tensor_copy(self.iota[:], self.iota_[:].bitcast(I32)))
            k.do(k.eng.tensor_copy(self.RWH[:], self.RW[:])); k.sync()
            k.do(k.eng.tensor_tensor(self.RWL[:], self.RW[:], self.RWH[:], ALU.subtract), T + "rws")
        self.transposed(k, T + "t", [T + "xn", "ident"], lambda i, t: self.XN[:, t, i * P:(i + 1) * P], None)
        ps = self.ps
        if k.name == "pe":
            k.wait(T + "t.split", T + "rws")
            for t in range(NT):
                n = 0
                for c in range(KT):
                    for xx, ww in ((self.XH, self.RWH), (self.XH, self.RWL), (self.XL, self.RWH), (self.XL, self.RWL)):
                        mm = k.eng.matmul(ps[:, 6, t * NE:(t + 1) * NE], xx[:, c, t * P:(t + 1) * P], ww[:, c, :], start=n == 0, stop=n == 4 * KT - 1)
                        n += 1
            k.do(mm, T + "lg")
        mo = self.mo
        v3 = lambda i: mo[:, 16 * i:16 * i + 16].rearrange("p (t e) -> p t e", t=NT)
        v1 = lambda i: mo[:, 288 + 2 * i:290 + 2 * i]
        bc = lambda a: a.rearrange("p (t o) -> p t o", o=1).broadcast_to([P, NT, NE])
        LG, A, B, OH1, OH2, SEL, G_, RI = (v3(i) for i in range(8))
        M1, M2, TM, W1, W2 = (v1(i) for i in range(5))
        POS = mo[:, 160:160 + 18].rearrange("p (t e) -> p t e", e=NE + 1)
        GATE = mo[:, 180:198].rearrange("p (t e) -> p t e", e=NE + 1)
        POS2 = mo[:, 200:218].rearrange("p (t e) -> p t e", e=NE + 1)
        CNT, FLAG = mo[:, 220:228], mo[:, 230:231].bitcast(I32)
        if k.name == "dve":
            def op(ins, *a):
                k.do(ins, *a); k.sync()
            tt, ts = k.eng.tensor_tensor, k.eng.tensor_scalar
            k.wait(T + "lg")
            op(k.eng.tensor_copy(LG, ps[:, 6, 0:16].rearrange("p (t e) -> p t e", t=NT)))
            for t in range(NT):
                op(ts(RI[:, t, :], self.iota[:, 0:NE], -1.0, float(NE), ALU.mult, ALU.add))
            def first_max(src, m, onehot):
                op(k.eng.tensor_reduce(m, src, AX, ALU.max))
                op(tt(A, src, bc(m), ALU.is_equal))
                op(tt(A, A, RI, ALU.mult))
                op(k.eng.tensor_reduce(TM, A, AX, ALU.max))
                op(tt(onehot, A, bc(TM), ALU.is_equal))
            first_max(LG, M1, OH1)
            op(k.eng.scalar_tensor_tensor(out=B, in0=OH1, scalar=-BIG, in1=LG, op0=ALU.mult, op1=ALU.add))
            first_max(B, M2, OH2)
            op(tt(W2, M2, M1, ALU.subtract), T + "w2")
        if k.name == "act":
            k.wait(T + "w2")
            k.do(k.eng.activation(W2, W2, ACT.Exp), T + "w2e")
        if k.name == "dve":
            k.wait(T + "w2e")
            op(ts(W1, W2, 1.0, None, ALU.add))
            op(k.eng.reciprocal(W1, W1))
            op(tt(W2, W2, W1, ALU.mult))
            op(k.eng.memset(mo[:, 160:220], 0.0))
            op(tt(A, OH1, bc(W1), ALU.mult))
            op(tt(B, OH2, bc(W2), ALU.mult))
            op(tt(GATE[:, :, 0:NE], A, B, ALU.add), T + "gate")
            op(tt(SEL, OH1, OH2, ALU.add), T + "sel")
        if k.name == "pe":
            k.wait(T + "sel", T + "ltri")
            o = ps[:, 7, :]
            k.eng.matmul(o[:, 0:NE], self.ltri[:, 0, :], SEL[:, 0, :], start=True, stop=True)
            k.eng.matmul(o[:, NE:2 * NE], self.ltri[:, 1, :], SEL[:, 0, :], start=True, stop=False)
            k.eng.matmul(o[:, NE:2 * NE], self.ltri[:, 0, :], SEL[:, 1, :], start=False, stop=True)
            k.eng.matmul(o[:, 2 * NE:3 * NE], self.ltri[:, 1, :], SEL[:, 0, :], start=True, stop=False)
            k.do(k.eng.matmul(o[:, 2 * NE:3 * NE], self.ltri[:, 1, :], SEL[:, 1, :], start=False, stop=True), T + "cum")
        if k.name == "dve":
            k.wait(T + "cum")
            op(ts(A, ps[:, 7, 0:16].rearrange("p (t e) -> p t e", t=NT), 1.0, None, ALU.add))
            op(tt(A, A, SEL, ALU.mult))
            op(ts(POS[:, :, 0:NE], A, -1.0, None, ALU.add))
            op(ts(POS[:, :, NE:], POS[:, :, NE:], 0.0, -1.0, ALU.mult, ALU.add))
            op(ts(POS2, POS, float(-P), None, ALU.add))
            op(k.eng.tensor_reduce(CNT[:, 0:1], ps[:, 7, 2 * NE:3 * NE], AX, ALU.max))
            op(ts(FLAG, CNT[:, 0:1], float(P), None, ALU.is_gt), T + "flag")
        self.experts(k, "x", POS, GATE)
        if k.name in ("pe", "act", "dve", "sp"):
            k.wait(T + "flag")
            more = k.eng.value_load(FLAG[0:1, :], min_val=0, max_val=1)
            with k.eng.If(more > 0):
                k.wait("x.end_pe", "x.end_act", "x.end_dve")
                with k.aside("again_", MOE_BASE):
                    self.feed(k, LEAD)
                    self.experts(k, "x2", POS2, GATE)
                    k.wait("x2.end_pe", "x2.end_act", "x2.end_dve")
        rs = self.rstd(k, "fin", lambda i: self.X[:, i, :], ["x.end_dve"], lambda i: self.XN[:, i, :])
        if k.name == "pool":
            k.wait("x.end_pe", "x.end_dve")
            k.dma(self.GB[:], self.a["final_norm"].rearrange("(o d) -> o d", o=1).broadcast_to([P, D]), "fin.g")
        if k.name == "dve":
            k.wait("fin.g")
            k.sync()
            for t in range(NT):
                k.do(k.eng.scalar_tensor_tensor(out=self.X[:, t, :], in0=self.X[:, t, :], scalar=rs[:, t:t + 1], in1=self.GB[:], op0=ALU.mult, op1=ALU.mult), "fin.out")

    def experts(self, k, T, POS, GATE):
        ps, XN = self.ps, self.XN
        gslot = self.small[:, 64:65]

        def slots(e, name):
            if k.name == "dve":
                for t in range(NT):
                    k.do(k.eng.tensor_scalar(self.PM[:, t, :], self.iota[:], POS[:, t, bass.ds(e, 1)], None, ALU.is_equal), f"{T}.pm{name}")

        def gather(name):
            if k.name == "pe":
                k.wait(f"{T}.pm{name}")
                for c in range(KT):
                    for t in range(NT):
                        mm = k.eng.matmul(ps[:, 6 + c // 4, (c % 4) * P:(c % 4 + 1) * P], XN[:, t, c * P:(c + 1) * P], self.PM[:, t, :], start=t == 0, stop=t == NT - 1)
                k.do(mm, f"{T}.ga{name}")
            for b in range(2):
                src = ps[:, 6 + b, :].rearrange("p (a b) -> p a b", a=4)
                to = lambda X: X[:, 4 * b:4 * b + 4, :]
                if k.name == "act":
                    k.wait(f"{T}.ga{name}")
                    k.do(k.eng.activation(to(self.XEH), src, ACT.Copy), f"{T}.xh{name}{b}")
                if k.name == "dve":
                    k.wait(f"{T}.xh{name}{b}")
                    k.do(k.eng.tensor_tensor(to(self.XEL), src, to(self.XEH), ALU.subtract), f"{T}.xl{name}")

        def scatter(name):
            if k.name == "pe":
                for t in range(NT):
                    for h in range(2):
                        o = ps[:, 4 + 2 * t + h, :]
                        k.eng.matmul(o, self.PT[:, t * P:(t + 1) * P], self.YH[:, h * CW:(h + 1) * CW], start=True, stop=False)
                        mm = k.eng.matmul(o, self.PT[:, t * P:(t + 1) * P], self.YL[:, h * CW:(h + 1) * CW], start=False, stop=True)
                k.do(mm, f"{T}.sc{name}")
            if k.name == "dve":
                k.wait(f"{T}.sc{name}")
                k.do(k.eng.tensor_tensor(self.X[:].rearrange("p t d -> p (t d)"), ps[:, 4:8, :].rearrange("p a b -> p (a b)"),
                                         self.X[:].rearrange("p t d -> p (t d)"), ALU.add), f"{T}.add{name}")

        if k.name == "dve":
            for G in (self.PT, self.YH, self.YL):
                k.do(k.eng.memset(G[:].bitcast(F32), 0.0), f"{T}.zero")
        slots(0, "0")
        gather("0")
        if k.name == "pe":
            k.wait(f"{T}.xl0", f"{T}.zero")
        with k.loop(T + ".experts", NE) as e:
            def first():
                if k.name == "pe":
                    k.wait(f"{T}.yl", back=1)
                scatter("L")
                if k.name == "pe":
                    for t in range(NT):
                        k.eng.transpose(ps[:, 3, t * P:(t + 1) * P], self.PM[:, t, :], self.ident[:])
                    for t in range(NT):
                        mm = k.eng.matmul(ps[:, 3, S:S + 1], self.PM[:, t, :], GATE[:, t, bass.ds(e, 1)], start=t == 0, stop=t == NT - 1)
                    k.do(mm, f"{T}.ptp")
                if k.name == "act":
                    k.wait(f"{T}.ptp")
                    k.do(k.eng.activation(self.PT[:], ps[:, 3, 0:S], ACT.Copy))
                    k.do(k.eng.activation(gslot, ps[:, 3, S:S + 1], ACT.Copy), f"{T}.pt")
                if k.name == "pe":
                    k.wait(f"{T}.pt")
                if k.name == "dve":
                    k.wait(f"{T}.ptp")
                slots(e + 1, "L")

            def in_down():
                gather("L")

            if k.name == "pe":
                k.wait(f"{T}.xlL", back=1)
            if k.name == "pe":
                pass
            self.ff(k, T + "f", 1, [], first, in_down)
            if k.name == "act":
                k.wait(f"{T}f.down")
                k.do(k.eng.activation(self.YH[:], ps[:, 4:6, :].rearrange("p a b -> p (a b)"), ACT.Copy, scale=gslot), f"{T}.yh")
            if k.name == "dve":
                k.wait(f"{T}.yh")
                k.do(k.eng.scalar_tensor_tensor(out=self.YL[:], in0=ps[:, 4:6, :].rearrange("p a b -> p (a b)"), scalar=gslot, in1=self.YH[:],
                                                op0=ALU.mult, op1=ALU.subtract), f"{T}.yl")
        if k.name == "pe":
            k.wait(f"{T}.yl")
        scatter("E")
        k.mark(f"{T}.end_{k.name}")

    def start2(self, k):
        L = 2 * S
        dist = self.TMPG[:, 0:4 * L].rearrange("p (h l) -> p h l", h=4)
        rbt, hot = self.TMPG[0:REL_BUCKETS, 4 * L:4 * L + 4], self.TMPG[0:REL_BUCKETS, 4 * L + 8:5 * L + 8]
        rbb = self.TMPG[0:REL_BUCKETS, 6 * L:7 * L].rearrange("p (h l) -> p h l", h=4)
        if k.name == "pool":
            k.wait("x.end_pe", "x.end_act", "x.end_dve")
            k.dma(rbt, self.a["rel_bias_2"], "rbt")
            k.dma(hot, self.a["bucket_of"], "hot")
            k.dma(self.MP[:], self.a["pool_windows"], "mp")
            k.do(k.eng.memset(self.ones[:], 1.0), "ones")
        if k.name == "dve":
            k.wait("rbt", "x.end_pe", "x.end_act")
            k.do(k.eng.tensor_copy(rbb, rbt.rearrange("p (h o) -> p h o", o=1).broadcast_to([REL_BUCKETS, 4, P])), "rbb")
        if k.name == "pe":
            k.wait("rbb", "hot", "x.end_dve")
            for h in range(4):
                mm = k.eng.matmul(self.ps[:, h, :], rbb[:, h, :], hot, start=True, stop=True)
            k.do(mm, "dist")
        if k.name == "act":
            k.wait("dist")
            k.do(k.eng.activation(dist, self.ps[:, 0:4, :], ACT.Copy), "distc")
        if k.name == "pool":
            k.wait("distc")
            skew = self.skew
            for h in range(4):
                k.do(k.eng.dma_start(skew[h, 0:P * L].rearrange("(p l) -> p l", p=P), dist[:, h, :]), "skewed", "d_skew", 16)
            k.wait("skewed")
            for t in range(NT):
                for h in range(4):
                    at = S - P * t
                    src = skew[h, at:at + P * (L - 1)].rearrange("(p l) -> p l", p=P)[:, 0:S]
                    k.do(k.eng.dma_start(self.RB[:, t, h, :], src), "rb", "d_rb", 16)

    def ff2(self, k, T, ready, pre, post, l):
        self.norm_in(k, T + "n", ready, pre)
        self.ff(k, T, NT, [T + "n.split"])
        self.post(k, T + "p", [T + ".down"], post, lambda t: self.ps[:, 4 * t:4 * t + 2, :].rearrange("p a b -> p (a b)"), 0.5, l)

    def post(self, k, T, ready, post, src, scale, l):
        gain = self.GP
        if k.name == "pool":
            k.wait(*ready)
            k.dma(gain[:], self.a[post][bass.ds(l, 1), :].broadcast_to([P, D]), T + "g")
        rs = self.rstd(k, T, src, ready, lambda i: self.XN[:, i, :])
        if k.name == "dve":
            k.wait(T + "g"); k.sync()
            for t in range(NT):
                k.do(k.eng.scalar_tensor_tensor(out=self.XN[:, t, :], in0=src(t), scalar=rs[:, t:t + 1], in1=gain[:], op0=ALU.mult, op1=ALU.mult))
            k.sync()
            for t in range(NT):
                k.do(k.eng.scalar_tensor_tensor(out=self.X[:, t, :], in0=self.XN[:, t, :], scalar=scale, in1=self.X[:, t, :], op0=ALU.mult, op1=ALU.add), T + "out")

    def layer2(self, k, l):
        pc = self.pc2
        col = lambda i: (lambda c: pc[:, i + c:i + c + 1])
        if k.name == "pool":
            k.dma(pc[:], self.a["pc2"][bass.ds(l, 1), :, :].rearrange("o p n -> p (o n)"), "pc2")
            k.dma(self.WS[:], self.a["gm_wsT"][bass.ds(l, 1), :, :, :].rearrange("o s g t -> s (o g) t"), "ws")
            k.dma(self.PW[0:64], self.a["pool_w_2"][bass.ds(l, 1), :, :, :].rearrange("o g c d -> c (o g) d"), "pw")
            k.dma(self.gvb[:], self.a["gm_v_g_2"][bass.ds(l, 1), :].broadcast_to([P, BW]), "gvb")
            k.wait("ws"); k.carry()
            k.do(k.eng.affine_select(out=self.WS[:], in_=self.WS[:], compare_op=ALU.is_ge, fill=0.0, base=0,
                                     pattern=[[0, 4], [1, P]], channel_multiplier=-1), "wsm")
        self.ff2(k, "g1", ["fin.out", "pc2", "rb"], col(0), "ffn1_post_g_2", l)
        if self.stop == "g1":
            return
        self.mixer2(k, l)
        if self.stop == "mx":
            return
        self.ff2(k, "g2", ["mxpout"], col(16), "ffn2_post_g_2", l)
        if k.name == "pool":
            k.wait("g2pout")

    def mixer2(self, k, l):
        ps, pc, sm = self.ps, self.pc2, self.small
        self.norm_in(k, "mxn", ["g1pout"], lambda c: pc[:, 8 + c:9 + c])
        Z = self.Z2[:].rearrange("p (n t c) -> p n t c", t=NT, c=CW)
        self.feed(k, 1)
        if k.name == "pe":
            k.wait("mxn.split")
            self.mm_slab(k, [(ps[:, 6 + t, 0:S], self.XH[:, c, t * P:(t + 1) * P], self.XL[:, c, t * P:(t + 1) * P],
                              slice(c * S, (c + 1) * S), c == 0, c == KT - 1) for t in range(NT) for c in range(KT)], event="mx.idx")
        QN, KN4 = self.LG[:, 0, :].rearrange("p (t c) -> p t c", t=NT), self.LG[:, 1, :].rearrange("p (t c) -> p t c", t=NT)
        WI = sm[:, 80:88].rearrange("p (t h) -> p t h", t=NT)
        if k.name == "act":
            k.wait("mx.idx")
            k.do(k.eng.activation(QN, ps[:, 6:8, 0:P], ACT.Copy))
            for t in range(NT):
                k.do(k.eng.activation(KN4[:, t, :].rearrange("p (r c) -> p r c", r=4),
                                      ps[:, 6 + t, P:P + 32].rearrange("p (o c) -> p o c", o=1).broadcast_to([P, 4, 32]), ACT.Copy))
            k.do(k.eng.activation(WI, ps[:, 6:8, P + 32:P + 36], ACT.Copy, scale=0.5), "mx.idxn")
        def evac(k, g, j, pair):
            if k.name == "act":
                k.wait(f"mx.mm{j}")
                k.do(k.eng.activation(self.Z2[:, bass.ds(g * (NT * CW), NT * CW)], ps[:, pair:pair + 2, :].rearrange("p a b -> p (a b)"), ACT.Copy), f"mx.ev{j}")
        self.groups(k, "mx", 12, evac)
        if k.name == "act":
            k.mark("mx.done")
        U, V = Z[:, 0, :, 0:BW], Z[:, 0, :, BW:]
        PP, Q = Z[:, 1, :, 0:BW], Z[:, 1, :, BW:]
        K, VA = Z[:, 2, :, 0:BW], Z[:, 2, :, BW:]
        A, GT = Z[:, 3, :, 0:BW], Z[:, 3, :, BW:]
        if k.name == "act":
            k.sync()
            k.do(k.eng.activation(Z[:, 0], Z[:, 0], ACT.Gelu_apprx_tanh), "mx.uv")
            k.do(k.eng.activation(GT, GT, ACT.Sigmoid), "mx.gt")
            k.do(k.eng.activation(Z[:, 4:12], Z[:, 4:12], ACT.Sigmoid), "mx.gates")
        XB = lambda T, n: T[:, 2 * n:2 * n + 2, :]

        HP, CA, CB = self.HP, self.CA, self.CB
        if k.name == "dve":
            k.wait("mx.gt")
            k.do(k.eng.tensor_tensor(A, A, GT, ALU.mult), "mx.h")
            k.do(k.eng.memset(HP[:, :, 0:30], 0.0))
        if k.name == "pe":
            k.wait("mx.h")
            for c in range(2):
                for t in range(NT):
                    mm = k.eng.transpose(ps[:, 0, c * S + t * P:c * S + (t + 1) * P], A[:, t, c * P:(c + 1) * P], self.ident[:])
            k.do(mm, "mx.ht")
        if k.name == "act":
            k.wait("mx.ht")
            k.do(k.eng.activation(HP[:, :, 30:], ps[:, 0, :].rearrange("p (c t) -> p c t", c=2), ACT.Copy), "mx.hp")
        dw = lambda c, j: pc[:, 24 + 31 * c + j:25 + 31 * c + j]
        cbias = lambda c: pc[:, 86 + c:87 + c]
        lng = lambda c: pc[:, 88 + c:89 + c]
        lnb = lambda c: pc[:, 90 + c:91 + c]
        if k.name == "dve":
            k.wait("mx.hp"); k.sync()
            for c in range(2):
                k.do(k.eng.tensor_scalar(CA[:, c, :], HP[:, c, 0:S], dw(c, 0), cbias(c), ALU.mult, ALU.add))
            for j in range(1, 31):
                k.sync()
                for c in range(2):
                    k.do(k.eng.scalar_tensor_tensor(out=CA[:, c, :], in0=HP[:, c, j:j + S], scalar=dw(c, j), in1=CA[:, c, :], op0=ALU.mult, op1=ALU.add), "mx.cv")
        def chansum(n, src, bank, ready):
            if k.name == "pe":
                k.wait(*ready)
                for c in range(2):
                    mm = k.eng.matmul(ps[:, bank, 0:S], self.ones[:], src[:, c, :], start=c == 0, stop=c == 1)
                k.do(mm, n)
        chansum("mx.s1", CA, 1, ["mx.cv", "ones"])
        if k.name == "dve":
            k.wait("mx.s1")
            for c in range(2):
                k.do(k.eng.scalar_tensor_tensor(out=CA[:, c, :], in0=ps[:, 1, 0:S], scalar=-1.0 / BW, in1=CA[:, c, :], op0=ALU.mult, op1=ALU.add))
            k.sync()
            k.do(k.eng.tensor_tensor(CB[:], CA[:], CA[:], ALU.mult), "mx.sq")
        chansum("mx.s2", CB, 2, ["mx.sq"])
        if k.name == "act":
            k.wait("mx.s2")
            k.do(k.eng.activation(CB[:, 0, :], ps[:, 2, 0:S], ACT.Sqrt, scale=1.0 / BW, bias=self.eps()), "mx.sd")
        if k.name == "dve":
            k.wait("mx.sd")
            k.do(k.eng.reciprocal(CB[:, 0, :], CB[:, 0, :])); k.sync()
            for c in range(2):
                k.do(k.eng.tensor_tensor(CA[:, c, :], CA[:, c, :], CB[:, 0, :], ALU.mult), "mx.ln")
        if k.name == "act":
            k.wait("mx.ln")
            for c in range(2):
                k.do(k.eng.activation(CA[:, c, :], CA[:, c, :], ACT.Silu, scale=lng(c), bias=lnb(c)))
            k.sync()
            k.do(k.eng.activation(XB(self.XH, 3), CA[:], ACT.Copy), "mx.b3h")
        if k.name == "dve":
            k.wait("mx.b3h")
            k.do(k.eng.tensor_tensor(XB(self.XL, 3), CA[:], XB(self.XH, 3), ALU.subtract), "mx.b3")

        ss, rs = sm[:, 96:98], sm[:, 98:100]
        if k.name == "act":
            k.wait("mx.b3")
            for t in range(NT):
                k.do(k.eng.activation(CB[:, t, :], V[:, t, :], ACT.Square, accum_out=ss[:, t:t + 1]))
            k.sync()
            k.do(k.eng.activation(rs, ss, ACT.Sqrt, scale=1.0 / BW, bias=self.eps()), "mx.vr")
        if k.name == "dve":
            k.wait("mx.vr", "gvb")
            k.do(k.eng.reciprocal(rs, rs)); k.sync()
            for t in range(NT):
                k.do(k.eng.scalar_tensor_tensor(out=V[:, t, :], in0=V[:, t, :], scalar=rs[:, t:t + 1], in1=self.gvb[:], op0=ALU.mult, op1=ALU.mult), "mx.v")
        if k.name == "pe":
            k.wait("mx.v", "wsm")
            for t in range(NT):
                for g in range(4):
                    mm = k.eng.matmul(ps[:, 3, t * BW + g * 64:t * BW + (g + 1) * 64], self.WS[:, g, :], V[:, t, g * 64:(g + 1) * 64], start=True, stop=True)
            k.do(mm, "mx.mix")
        if k.name == "dve":
            k.wait("mx.mix")
            wb = pc[:, 92:96].rearrange("p (g o) -> p g o", o=1).broadcast_to([P, 4, 64])
            for t in range(NT):
                k.do(k.eng.tensor_tensor(V[:, t, :].rearrange("p (g d) -> p g d", g=4), ps[:, 3, t * BW:(t + 1) * BW].rearrange("p (g d) -> p g d", g=4), wb, ALU.add))
            k.sync()
            k.do(k.eng.tensor_tensor(U, U, V, ALU.mult), "mx.g")
        self.transposed(k, "mxg", ["mx.g"], lambda i, t: U[:, t, i * P:(i + 1) * P], None, n=2, at=0, bank0=4)

        DT = self.QI[0:64]
        for half in range(2):
            if k.name == "pe":
                k.wait("mp", "pw", "mx.done") if half == 0 else k.wait("mx.dt0")
                for i in range(2):
                    g = 2 * half + i
                    o = ps[0:64, 5, i * S:(i + 1) * S]
                    k.eng.matmul(o, PP[:, 0, g * 64:(g + 1) * 64], self.MP[:, g, 0:S], start=True, stop=False, skip_group_check=True)
                    mm = k.eng.matmul(o[:, P:], PP[:, 1, g * 64:(g + 1) * 64], self.MP[:, g, S:], start=False, stop=True, skip_group_check=True)
                k.do(mm, f"mx.d{half}")
            if k.name == "act":
                k.wait(f"mx.d{half}")
                if half:
                    k.wait("mx.pj0")
                k.do(k.eng.activation(DT, ps[0:64, 5, :].rearrange("p (a b) -> p a b", a=2), ACT.Copy), f"mx.dt{half}")
            if k.name == "pe":
                k.wait(f"mx.dt{half}")
                k.carry()
                for i in range(2):
                    g = 2 * half + i
                    mm = k.eng.matmul(ps[i * 64:(i + 1) * 64, 6, half * S:(half + 1) * S], self.PW[0:64, g, :], DT[:, i, :], start=True, stop=True)
                k.do(mm, f"mx.pj{half}")
        self.split_into(k, "mxpl", ["mx.pj1"], *[(ps[:, 6, c * S:(c + 1) * S], self.XH[:, 2 + c, :], self.XL[:, 2 + c, :], pc[:, 96 + c:97 + c]) for c in range(2)])

        self.attention(k, Q, K, VA, QN, KN4, WI)

        Y = self.XN[:].rearrange("p t (h c) -> p t h c", h=2)
        TM = Z[:, 0:2].rearrange("p n t c -> p (n t c)").rearrange("p (t h c) -> p t h c", t=NT, h=2)
        for n in range(4):
            banks = ((0, 1), (2, 3)) if n % 2 == 0 else ((4, 5), (6, 7))
            self.feed(k, 1)
            if k.name == "pe":
                k.wait("mx.b3", "mxg.split", "mxpl.l", "at.split") if n == 0 else None
                if n >= 2:
                    k.wait(f"mx.y{n - 2}")
                self.mm_slab(k, [(ps[:, banks[t][h], :], self.XH[:, 2 * n + c, t * P:(t + 1) * P], self.XL[:, 2 * n + c, t * P:(t + 1) * P],
                                  slice(c * D + h * CW, c * D + (h + 1) * CW), c == 0, c == 1) for t in range(NT) for c in range(2) for h in range(2)], event=f"mx.br{n}")
            if k.name == "dve":
                k.wait(f"mx.br{n}", "mx.gates")
                for t in range(NT):
                    acc = ps[:, banks[t][0]:banks[t][0] + 2, :]
                    gate = Z[:, 4 + 2 * n:6 + 2 * n, t, :]
                    k.do(k.eng.tensor_tensor(Y[:, t] if n == 0 else TM[:, t], acc, gate, ALU.mult), f"mx.y{n}")
                k.sync()
                if n:
                    k.do(k.eng.tensor_tensor(Y, Y, TM, ALU.add), "mx.Y")
                    k.sync()
        self.transposed(k, "mxy", ["mx.Y"], lambda i, t: self.XN[:, t, i * P:(i + 1) * P], None, bank0=0)
        self.groups(k, "mxo", 2, lambda *a: None, per=2, ready=["mxy.split"])
        self.post(k, "mxp", ["mxo.mm1"], "mix_post_g_2", lambda t: ps[:, t:t + 3:2, :], 1.0, l)

    def attention(self, k, Q, K, VA, QN, KN4, WI):
        ps, Z = self.ps, self.Z2
        QT, KTT, QI, LG, SCO, WRK, m8 = self.QT, self.KTT, self.QI, self.LG, self.SCO, self.WRK, self.m8
        if k.name == "pe":
            k.wait("mx.idxn", "mx.done", "mx.g", "mxg.split", "mxpl.l")
            for i, src in enumerate((QN, KN4)):
                for t in range(NT):
                    mm = k.eng.transpose(ps[:, 0, i * S + t * P:i * S + (t + 1) * P], src[:, t, :], self.ident[:])
            for i, src in enumerate((Q, K)):
                for c in range(2):
                    for t in range(NT):
                        mm = k.eng.transpose(ps[:, 1 + i, c * S + t * P:c * S + (t + 1) * P], src[:, t, c * P:(c + 1) * P], self.ident[:])
            k.do(mm, "at.t")
        if k.name == "act":
            k.wait("at.t", "mx.pj1")
            k.do(k.eng.activation(QI[:], ps[:, 0, :].rearrange("p (c t) -> p c t", c=2), ACT.Copy))
            k.do(k.eng.activation(QT[:], ps[:, 1, :].rearrange("p (c t) -> p c t", c=2), ACT.Copy))
            k.do(k.eng.activation(KTT[:], ps[:, 2, :].rearrange("p (c t) -> p c t", c=2), ACT.Copy), "at.tc")
        PTB = self.XN[:].rearrange("p t d -> p (t d)")
        for t in range(NT):
            e = lambda n: f"at.{n}{t}"
            if k.name == "pe":
                k.wait("at.tc") if t == 0 else k.wait("at.rel0", "at.lg0")
                k.carry()
                for h in range(4):
                    r = slice(32 * h, 32 * (h + 1))
                    mm = k.eng.matmul(ps[:, 1 + h, 0:S], QI[r, 0, t * P:(t + 1) * P], QI[r, 1, :], start=True, stop=True)
                k.do(mm, e("ip"))
                for h in range(4):
                    r = slice(64 * (h % 2), 64 * (h % 2 + 1))
                    mm = k.eng.matmul(ps[:, 5 + h % 2, (h // 2) * S:(h // 2 + 1) * S], QT[r, h // 2, t * P:(t + 1) * P], KTT[r, h // 2, :], start=True, stop=True)
                k.do(mm, e("qk"))
            REL = LG
            if k.name == "act":
                k.wait(e("ip"))
                if t:
                    k.wait("at.pT0")
                k.do(k.eng.activation(REL[:], ps[:, 1:5, 0:S], ACT.Relu, scale=32.0 ** -0.5), e("rel"))
            S0, NM = SCO[:, 0, :], SCO[:, 1, :]
            W = WRK[:, 0, :]
            if k.name == "dve":
                k.wait(e("rel"))
                k.do(k.eng.tensor_scalar(S0, REL[:, 0, :], WI[:, t, 0:1], None, ALU.mult)); k.sync()
                for h in range(1, 4):
                    k.do(k.eng.scalar_tensor_tensor(out=S0, in0=REL[:, h, :], scalar=WI[:, t, h:h + 1], in1=S0, op0=ALU.mult, op1=ALU.add), e("s0")); k.sync()
            if k.name == "pool":
                k.wait(e("s0")); k.carry()
                k.do(k.eng.affine_select(out=S0, in_=S0, compare_op=ALU.is_ge, fill=-BIG, base=t * P, pattern=[[-1, S]], channel_multiplier=1), e("s1"))
            if k.name == "dve":
                k.wait(e("s1"))
                k.do(k.eng.tensor_copy(W, S0)); k.sync()
                for r in range(TOPK // 8):
                    k.carry()
                    k.do(k.eng.max(m8[:, 0:8], W)); k.sync(); k.carry()
                    k.do(k.eng.match_replace(W, m8[:, 0:8], W, -3.3e38)); k.sync()
                k.do(k.eng.tensor_scalar(NM, W, -3.2e38, -BIG, ALU.is_gt, ALU.mult), e("n0"))
            if k.name == "pool":
                k.wait(e("n0")); k.carry()
                k.do(k.eng.affine_select(out=NM, in_=NM, compare_op=ALU.is_ge, fill=-BIG, base=t * P, pattern=[[-1, S]], channel_multiplier=1), e("n1"))
            mx, sums = m8[:, 8:12], m8[:, 12:16]
            if k.name == "dve":
                k.wait(e("qk"), "rb")
                for r in range(2):
                    k.do(k.eng.scalar_tensor_tensor(out=LG[:, r:4:2, :], in0=ps[:, 5 + r, :].rearrange("p (b c) -> p b c", b=2), scalar=0.125, in1=self.RB[:, t, r:4:2, :], op0=ALU.mult, op1=ALU.add), e("lg"))
                k.wait(e("n1")); k.sync()
                k.do(k.eng.tensor_tensor(LG[:], LG[:], NM.rearrange("p (o c) -> p o c", o=1).broadcast_to([P, 4, S]), ALU.add)); k.sync()
                k.do(k.eng.tensor_reduce(mx, LG[:], AX, ALU.max)); k.sync()
                k.do(k.eng.tensor_tensor(LG[:], LG[:], mx.rearrange("p (h o) -> p h o", o=1).broadcast_to([P, 4, S]), ALU.subtract), e("lm"))
            if k.name == "act":
                k.wait(e("lm"))
                k.do(k.eng.activation(LG[:], LG[:], ACT.Exp), e("ex"))
            if k.name == "dve":
                k.wait(e("ex"))
                k.do(k.eng.tensor_reduce(sums, LG[:], AX, ALU.add)); k.sync()
                k.do(k.eng.reciprocal(sums, sums)); k.sync()
                k.do(k.eng.tensor_tensor(LG[:], LG[:], sums.rearrange("p (h o) -> p h o", o=1).broadcast_to([P, 4, S]), ALU.mult), e("p"))
            if k.name == "pe":
                k.wait(e("p"))
                for s in range(t + 1):
                    for h in range(4):
                        mm = k.eng.transpose(ps[:, 7 * s, h * P:(h + 1) * P], LG[:, h, s * P:(s + 1) * P], self.ident[:])
                k.do(mm, e("pT"))
            if k.name == "act":
                k.wait(e("pT"))
                pt = PTB.rearrange("p (s h q) -> p s h q", s=2, h=4)
                for s in range(t + 1):
                    k.do(k.eng.activation(pt[:, s, :, t * P:(t + 1) * P], ps[:, 7 * s, :].rearrange("p (h q) -> p h q", h=4), ACT.Copy), e("pt"))
        if k.name == "pe":
            k.wait("at.pt1")
            pt = PTB.rearrange("p (s h q) -> p s h q", s=2, h=4)
            for h in range(4):
                o = ps[64 * (h % 2):64 * (h % 2) + 64, 5, (h // 2) * S:(h // 2 + 1) * S]
                k.eng.matmul(o, VA[:, 0, h * 64:(h + 1) * 64], pt[:, 0, h, :], start=True, stop=False, skip_group_check=True)
                mm = k.eng.matmul(o[:, P:], VA[:, 1, h * 64:(h + 1) * 64], pt[:, 1, h, P:], start=False, stop=True, skip_group_check=True)
            k.do(mm, "at.o")
        self.split_into(k, "at", ["at.o"], (ps[:, 5, :].rearrange("p (c t) -> p c t", c=2), self.XH[:, 4:6, :], self.XL[:, 4:6, :], None))
        if k.name == "dve":
            k.mark("at.split")

    def program(self, k):
        stop = self.stop
        def dump(*ready):
            if k.name == "sp":
                k.wait(*ready)
                k.dma(self.out.rearrange("(t p) d -> p t d", p=P), self.X[:], "stored")
                k.wait("stored")
        self.start(k)
        self.mixer1(k, 0)
        if stop == "m0":
            return dump("m0.out")
        self.ffn1(k)
        if stop == "f0":
            return dump("f0.out")
        self.mixer1(k, 1)
        if stop == "m1":
            return dump("m1.out")
        self.moe(k)
        if stop == "moe":
            return dump("fin.out")
        self.start2(k)
        with k.loop("layer", 1 if stop else 2) as l:
            self.layer2(k, l)
        dump({"g1": "g1pout", "mx": "mxpout"}.get(stop, "g2pout"))


def build(make, args, out, stop=None):
    memo = Memo()
    for last in (False, False, True):
        memo.last = last
        nc, a, o = make()
        kern = Kernel(nc, a, o, memo, stop)
        kern.skew = nc.dram_tensor("skew", (4, P * 2 * S + 2 * S), F32).ap()
        with kern.stack:
            kern.memory()
            with nc.Block() as block:
                for name, on in (("sp", block.sync), ("pool", block.gpsimd), ("act", block.scalar), ("dve", block.vector), ("pe", block.tensor)):
                    @on
                    def _(eng, name=name):
                        kern.program(Core(name, eng, kern.sem, memo))
    return nc


def level_tables():
    s, t = np.arange(P)[:, None], np.arange(P)[None, :]
    mats, masks = [], []
    for m in LEVELS:
        same = s // (2 * m) == t // (2 * m)
        first = (t // m) % 2 == 0
        mats.append(np.where(first, same & ((s // m) % 2 == 0) & (s > t), same & ((s // m) % 2 == 1) & (s <= t)))
        masks.append(same & ((s // m) % 2 == 0) & ((t // m) % 2 == 1))
    a, b = s > t, s <= t
    cum = np.concatenate(mats[:4] + mats[4:] + [a] + mats[4:] + [b], 1).astype(np.float32)
    return cum, np.stack(masks, 1).astype(np.float32)


def pool_table():
    out = np.zeros((S, 4, S), np.float32)
    for g, w in enumerate((2, 4, 8, 16)):
        for t in range(S):
            out[max(0, t - w + 1):t + 1, g, t] = 1.0 / min(t + 1, w)
            out[t, g, t] -= 1.0
    return np.concatenate([out[:P], out[P:, :, P:]], 2)


def bucket_table():
    n = np.maximum(S - np.arange(2 * S), 0)
    half = REL_BUCKETS // 2
    large = half + (np.log(np.maximum(n, 1).astype(np.float32) / np.float32(half)) / np.float32(np.log(128 / half)) * np.float32(REL_BUCKETS - half)).astype(np.int32)
    b = np.where(n < half, n, np.minimum(large, REL_BUCKETS - 1))
    return (b[None, :] == np.arange(REL_BUCKETS)[:, None]).astype(np.float32)


def column_slabs(w):
    n = w.shape[1] // CW
    return w.reshape(2, 4, P, n, CW).transpose(3, 0, 2, 1, 4).reshape(2 * n, P, SLAB)


def row_slabs(w):
    return w.reshape(-1, 2, P, D).transpose(0, 2, 1, 3).reshape(-1, P, SLAB)


def gate_up(a, b):
    return np.stack([a.reshape(D, FF_GROUPS, BW), b.reshape(D, FF_GROUPS, BW)], 2).reshape(D, 2 * FF)


def feed_forward(a, b, w):
    return [column_slabs(gate_up(a, b)), row_slabs(w)]


def stream(i):
    parts = []
    q = {n: i["w_in"][:, :, n * D:(n + 1) * D] for n in range(9)}
    for l in range(2):
        parts.append(column_slabs(np.concatenate([q[n][l] for n in (1, 2, 0, 3, 4, 5, 6, 7, 8)], 1)))
        parts += [column_slabs(i[n][l]) for n in ("w_proj_hgrn", "w_proj_conv", "w_out")]
        if l == 0:
            parts += feed_forward(i["dense_w1"][0], i["dense_w3"][0], i["dense_w2"][0])
        else:
            for e in range(NE):
                parts += feed_forward(i["expert_w1"][0, e], i["expert_w3"][0, e], i["expert_w2"][0, e])
    for l in range(2):
        for n in (1, 2):
            gu = i[f"ffn{n}_w_gu_2"][l]
            if n == 2:
                w = i["w_in_2"][l]
                at = 6 * BW
                rest = np.concatenate([w[:, at:at + REST], np.zeros((D, S - REST), np.float32)], 1)
                parts.append(rest.reshape(KT, P, S).transpose(1, 0, 2).reshape(1, P, SLAB))
                parts.append(column_slabs(np.concatenate([w[:, :at], w[:, at + REST:]], 1)))
                parts.append(row_slabs(i["w_branch_2"][l].reshape(4 * BW, D)))
                parts.append(column_slabs(i["w_out_2"][l]))
            parts += feed_forward(gu[:, :FF], gu[:, FF:], i[f"ffn{n}_w_down_2"][l])
    parts.append(np.zeros((LEAD, P, SLAB), np.float32))
    return np.concatenate(parts)


def kernel(**inputs):
    import concourse.bacc as bacc
    from concourse.bass_utils import run_bass_kernel_spmd

    i = {n: np.asarray(a) for n, a in inputs.items()}
    cols = lambda v: v.reshape(-1, P).T
    cum, masks = level_tables()
    arrays = {
        "W": stream(i),
        "x": i["x"][0],
        "pcols": np.concatenate([np.concatenate([cols(i["norm_mix"][l]), cols(i["norm_ffn"][l]), cols(i["hgrn_norm_w"][l]),
                                                 cols(i["conv_w"][l])], 1) for l in range(2)], 1),
        "lower_bounds": i["lower_bounds"], "norm_ffn": i["norm_ffn"], "final_norm": i["final_norm"], "router_w": i["router_w"],
        "cum_sums": cum, "level_masks": masks, "pool_windows": pool_table(), "bucket_of": bucket_table(),
        "rel_bias_2": i["rel_bias_2"], "gm_wsT": i["gm_ws_2"].transpose(0, 3, 1, 2), "pool_w_2": i["pool_w_2"], "gm_v_g_2": i["gm_v_g_2"],
        "ffn1_post_g_2": i["ffn1_post_g_2"], "mix_post_g_2": i["mix_post_g_2"], "ffn2_post_g_2": i["ffn2_post_g_2"],
        "pc2": np.stack([np.concatenate([cols(i["ffn1_pre_g_2"][l]), cols(i["mix_pre_g_2"][l]), cols(i["ffn2_pre_g_2"][l]),
                                         i["conv_dw_2"][l].reshape(31, 2, P).transpose(2, 1, 0).reshape(P, 62), cols(i["conv_b_2"][l]),
                                         cols(i["conv_ln_g_2"][l]), cols(i["conv_ln_b_2"][l]), i["gm_b_2"][l].T, cols(i["pool_scale_2"][l])], 1)
                         for l in range(2)]),
    }
    arrays = {n: np.ascontiguousarray(a) for n, a in arrays.items()}

    def make():
        nc = bacc.Bacc("TRN2", target_bir_lowering=False, num_devices=1)
        a = {n: nc.dram_tensor(f"in_{n}", v.shape, mybir.dt.from_np(v.dtype), kind="ExternalInput").ap() for n, v in arrays.items()}
        return nc, a, nc.dram_tensor("out", (S, D), F32, kind="ExternalOutput").ap()

    nc = build(make, None, None, STOP)
    r = run_bass_kernel_spmd(nc, [{f"in_{n}": v for n, v in arrays.items()}], core_ids=[0])
    return r.results[0]["out"].reshape(1, S, D)


STOP = None
```
